# Optimizing a Trainium2 kernel written in Bass

```python
import functools
import jax
import jax.numpy as jnp
from jax import lax
import numpy as np

D_MODEL = 1024
BATCH = 1
SEQ = 512
DEPTH = 2
DEC_BATCH = 8
DEC_SEQ = 4
PAST_LEN = 1024
PAGE_SIZE = 128

CHUNK_A = 128
G_A = 4
DG_A = 128
D_A = G_A * DG_A
H_B = 8
DH_B = 64
D_B = H_B * DH_B
Q_BLOCK = 128
H_C = 4
DK_C = 64
DV_C = 128
DQK_C = H_C * DK_C
D_C = H_C * DV_C
CHUNK_C = 128
N_BRANCH = 3
BRANCH_W = 512
N_SUB = 3
D_FF = 2816
FFN_RES = 0.5
EPS = 1e-6
FORGET_BIAS = 3.0
IN_SPLITS = (D_A, D_A, D_B, D_B, D_B, H_B, DQK_C, DQK_C, D_C, H_C, H_C, D_C, N_BRANCH * D_MODEL)
D_IN = 2 * D_A + 3 * D_B + H_B + 2 * DQK_C + 2 * D_C + 2 * H_C + N_BRANCH * D_MODEL

kernel_name = 'hybrid_fox_mlstm_chunkmlp_step'

def rmsnorm(x, g):
    xf = x.astype(jnp.float32)
    y = xf * lax.rsqrt(jnp.mean(xf * xf, axis=-1, keepdims=True) + EPS)
    return (y * g.astype(jnp.float32)).astype(x.dtype)

def modulated_norm(x, g, shift, scale):
    return rmsnorm(x, g) * (1 + scale[:, None]) + shift[:, None]

def half_ffn(x, mod, g, w_up, w_down):
    h = modulated_norm(x, g, mod[:, 0], mod[:, 1])
    a, b = jnp.split(h @ w_up, 2, axis=-1)
    return x + FFN_RES * mod[:, 2][:, None] * ((jax.nn.silu(a) * b) @ w_down)

def project_in(h, w_in, g_va, g_qb, g_kb, b_fb, b_ic, b_fc):
    B, L, _ = h.shape
    points = np.cumsum(IN_SPLITS)[:-1].tolist()
    ua, va, qb, kb, vb, fb, qc, kc, vc, ic, fc, oc, gt = jnp.split(h @ w_in, points, axis=-1)
    ua = jax.nn.gelu(ua)
    va = rmsnorm(jax.nn.gelu(va), g_va)
    qb = rmsnorm(qb.reshape(B, L, H_B, DH_B), g_qb)
    kb = rmsnorm(kb.reshape(B, L, H_B, DH_B), g_kb)
    vb = vb.reshape(B, L, H_B, DH_B)
    lfb = jax.nn.log_sigmoid((fb + b_fb).astype(jnp.float32))
    qc = qc.reshape(B, L, H_C, DK_C)
    kc = kc.reshape(B, L, H_C, DK_C) * (DK_C ** -0.5)
    vc = vc.reshape(B, L, H_C, DV_C)
    ic = (ic + b_ic).astype(jnp.float32)
    lfc = jax.nn.log_sigmoid((fc + b_fc).astype(jnp.float32))
    oc = jax.nn.sigmoid(oc)
    gates = jax.nn.sigmoid(gt).reshape(B, L, N_BRANCH, D_MODEL)
    return ua, va, qb, kb, vb, lfb, qc, kc, vc, ic, lfc, oc, gates

def spatial_gate(u, v, w_s, b_s):
    B, S, _ = v.shape
    L = min(S, CHUNK_A)
    nc = S // L
    w = jnp.where(jnp.tril(jnp.ones((L, L), bool)), w_s[:, :L, :L], 0.0)
    vc = v.reshape(B, nc, L, G_A, DG_A)
    mix = jnp.einsum('gts,bnsgc->bntgc', w, vc) + b_s[:, :L].T[None, None, :, :, None]
    return u * mix.reshape(B, S, D_A)

def fox_block(q, k, v, fq, fk, qpos, kpos):
    s = jnp.einsum('bqhd,bkhd->bhqk', q.astype(jnp.float32), k) * (DH_B ** -0.5)
    s = s + (jnp.swapaxes(fq, 1, 2)[..., :, None] - jnp.swapaxes(fk, 1, 2)[..., None, :])
    s = jnp.where(kpos[None, None, None, :] <= qpos[None, None, :, None], s, -jnp.inf)
    p = jax.nn.softmax(s, axis=-1)
    return jnp.einsum('bhqk,bkhd->bqhd', p, v)

def fox_prompt(q, k, v, logf):
    B, S, H, _ = q.shape
    nb = S // Q_BLOCK
    F = jnp.cumsum(logf, axis=1)
    kpos = jnp.arange(S)
    kf = k.astype(jnp.float32)
    vf = v.astype(jnp.float32)

    def block(args):
        qblk, fblk, qpos = args
        return fox_block(qblk, kf, vf, fblk, F, qpos, kpos)

    qs = q.reshape(B, nb, Q_BLOCK, H, DH_B).swapaxes(0, 1)
    fs = F.reshape(B, nb, Q_BLOCK, H).swapaxes(0, 1)
    ps = kpos.reshape(nb, Q_BLOCK)
    out = lax.map(block, (qs, fs, ps))
    return out.swapaxes(0, 1).reshape(B, S, D_B).astype(v.dtype)

def fox_sample(q, k_new, v_new, lf_new, k_pages, v_pages, lf_pages):
    Bd, n_pages = k_pages.shape[:2]
    past = n_pages * PAGE_SIZE
    L = q.shape[1]
    k = jnp.concatenate([k_pages.reshape(Bd, past, H_B, DH_B), k_new], axis=1).astype(jnp.float32)
    v = jnp.concatenate([v_pages.reshape(Bd, past, H_B, DH_B), v_new], axis=1).astype(jnp.float32)
    lf = jnp.concatenate([lf_pages.reshape(Bd, past, H_B).astype(jnp.float32), lf_new], axis=1)
    F = jnp.cumsum(lf, axis=1)
    kpos = jnp.arange(past + L)
    out = fox_block(q, k, v, F[:, past:], F, kpos[past:], kpos)
    return out.reshape(Bd, L, D_B).astype(v_new.dtype)

def mlstm_chunk(carry, xs):
    C, n, m = carry
    q, k, v, ig, lf = xs
    L = q.shape[1]
    b = jnp.cumsum(lf, axis=1).swapaxes(1, 2)
    i = ig.swapaxes(1, 2)
    causal = jnp.tril(jnp.ones((L, L), bool))
    dmat = jnp.where(causal, b[..., :, None] - b[..., None, :] + i[..., None, :], -jnp.inf)
    inter = b + m[..., None]
    m_t = jnp.maximum(jnp.max(dmat, axis=-1), inter)
    w_intra = jnp.exp(dmat - m_t[..., None]) * jnp.einsum('blhd,bshd->bhls', q, k)
    w_inter = jnp.exp(inter - m_t)
    num = jnp.einsum('bhls,bshv->bhlv', w_intra, v) + w_inter[..., None] * jnp.einsum('bhvd,blhd->bhlv', C, q)
    den = jnp.sum(w_intra, axis=-1) + w_inter * jnp.einsum('bhd,blhd->bhl', n, q)
    h = num / jnp.maximum(jnp.abs(den), jnp.exp(-m_t))[..., None]
    m_new = m_t[..., -1]
    w_k = jnp.exp(b[..., -1:] - b + i - m_new[..., None])
    decay = jnp.exp(b[..., -1] + m - m_new)
    C_new = decay[..., None, None] * C + jnp.einsum('bhs,bshv,bshd->bhvd', w_k, v, k)
    n_new = decay[..., None] * n + jnp.einsum('bhs,bshd->bhd', w_k, k)
    return (C_new, n_new, m_new), h.swapaxes(1, 2)

def mlstm_prompt(q, k, v, ig, lf):
    B, S = q.shape[:2]
    nc = S // CHUNK_C

    def to_chunks(a):
        return a.astype(jnp.float32).reshape((B, nc, CHUNK_C) + a.shape[2:]).swapaxes(0, 1)

    init = (jnp.zeros((B, H_C, DV_C, DK_C), jnp.float32), jnp.zeros((B, H_C, DK_C), jnp.float32),
            jnp.zeros((B, H_C), jnp.float32))
    state, h = lax.scan(mlstm_chunk, init, (to_chunks(q), to_chunks(k), to_chunks(v), to_chunks(ig), to_chunks(lf)))
    return state, h.swapaxes(0, 1).reshape(B, S, D_C)

def prompt_mix(qb, kb, vb, lfb, qc, kc, vc, ic, lfc):
    yb = fox_prompt(qb, kb, vb, lfb)
    (C, n, m), hc = mlstm_prompt(qc, kc, vc, ic, lfc)
    return yb, hc.astype(vc.dtype), (kb, vb, lfb, C, n, m)

def sample_mix(qb, kb, vb, lfb, qc, kc, vc, ic, lfc, *, layer, cache_k, cache_v, cache_logf,
               page_table, state_C, state_n, state_m):
    yb = fox_sample(qb, kb, vb, lfb, cache_k[layer, page_table], cache_v[layer, page_table],
                    cache_logf[layer, page_table])
    carry = (state_C[layer].astype(jnp.float32), state_n[layer].astype(jnp.float32),
             state_m[layer].astype(jnp.float32))
    f32 = jnp.float32
    (C, n, m), hc = mlstm_chunk(carry, (qc.astype(f32), kc.astype(f32), vc.astype(f32), ic, lfc))
    B, L = qc.shape[:2]
    return yb, hc.reshape(B, L, D_C).astype(vc.dtype), (kb, vb, lfb, C, n, m)

def merge_branches(ys, gates, w_branch, w_out):
    m = gates[:, :, 0] * (ys[0] @ w_branch[0])
    for nb in range(1, N_BRANCH):
        m = m + gates[:, :, nb] * (ys[nb] @ w_branch[nb])
    return m @ w_out

def trunk_layer(x, c, lw, token_mix):
    (w_ada, b_ada, g_norm, w_ff_up, w_ff_down, w_in, g_va, w_s, b_s,
     g_qb, g_kb, b_fb, b_ic, b_fc, w_branch, w_out) = lw
    mod = (jax.nn.silu(c) @ w_ada + b_ada).reshape(c.shape[0], N_SUB, 3, D_MODEL)
    x = half_ffn(x, mod[:, 0], g_norm[0], w_ff_up[0], w_ff_down[0])
    h = modulated_norm(x, g_norm[1], mod[:, 1, 0], mod[:, 1, 1])
    ua, va, qb, kb, vb, lfb, qc, kc, vc, ic, lfc, oc, gates = project_in(h, w_in, g_va, g_qb, g_kb, b_fb, b_ic, b_fc)
    ya = spatial_gate(ua, va, w_s, b_s)
    yb, hc, state = token_mix(qb, kb, vb, lfb, qc, kc, vc, ic, lfc)
    yc = oc * hc
    x = x + mod[:, 1, 2][:, None] * merge_branches((ya, yb, yc), gates, w_branch, w_out)
    x = half_ffn(x, mod[:, 2], g_norm[2], w_ff_up[1], w_ff_down[1])
    return x, va, state

def setup_inputs(seed: int = 0) -> dict:
    key = jax.random.key(seed)
    ks = list(jax.random.split(key, 32))
    n_pages = PAST_LEN // PAGE_SIZE
    n_used = DEC_BATCH * n_pages
    n_pool = (n_used * 5) // 4

    def nrm(i, shape, scale):
        return scale * jax.random.normal(ks[i], shape, jnp.float32)

    x_prompt = nrm(0, (BATCH, SEQ, D_MODEL), 1.0)
    x_sample = nrm(1, (DEC_BATCH, DEC_SEQ, D_MODEL), 1.0)
    cache_k = nrm(2, (DEPTH, n_pool, PAGE_SIZE, H_B, DH_B), 1.0)
    cache_v = nrm(3, (DEPTH, n_pool, PAGE_SIZE, H_B, DH_B), 1.0)
    cache_logf = jax.nn.log_sigmoid(FORGET_BIAS + nrm(4, (DEPTH, n_pool, PAGE_SIZE, H_B), 1.0))
    state_C = nrm(5, (DEPTH, DEC_BATCH, H_C, DV_C, DK_C), 0.3)
    state_n = nrm(6, (DEPTH, DEC_BATCH, H_C, DK_C), 0.3)
    state_m = nrm(7, (DEPTH, DEC_BATCH, H_C), 1.0)
    page_table = jax.random.permutation(ks[8], n_pool)[:n_used].reshape(DEC_BATCH, n_pages).astype(jnp.int32)
    c_prompt = nrm(9, (BATCH, D_MODEL), 1.0)
    c_sample = nrm(10, (DEC_BATCH, D_MODEL), 1.0)
    w_ada = nrm(11, (DEPTH, D_MODEL, N_SUB * 3 * D_MODEL), 0.5 * D_MODEL ** -0.5)
    b_ada = nrm(12, (DEPTH, N_SUB * 3 * D_MODEL), 0.02)
    g_norm = 1.0 + nrm(13, (DEPTH, N_SUB, D_MODEL), 0.1)
    w_ff_up = nrm(14, (DEPTH, 2, D_MODEL, 2 * D_FF), D_MODEL ** -0.5)
    w_ff_down = nrm(15, (DEPTH, 2, D_FF, D_MODEL), D_FF ** -0.5)
    w_in = nrm(16, (DEPTH, D_MODEL, D_IN), D_MODEL ** -0.5)
    g_va = 1.0 + nrm(17, (DEPTH, D_A), 0.1)
    w_s = nrm(18, (DEPTH, G_A, CHUNK_A, CHUNK_A), CHUNK_A ** -0.5)
    b_s = 1.0 + nrm(19, (DEPTH, G_A, CHUNK_A), 0.1)
    g_qb = 1.0 + nrm(20, (DEPTH, DH_B), 0.1)
    g_kb = 1.0 + nrm(21, (DEPTH, DH_B), 0.1)
    b_fb = FORGET_BIAS + nrm(22, (DEPTH, H_B), 0.5)
    b_ic = nrm(23, (DEPTH, H_C), 0.1)
    b_fc = FORGET_BIAS + nrm(24, (DEPTH, H_C), 0.5)
    w_branch = nrm(25, (DEPTH, N_BRANCH, BRANCH_W, D_MODEL), BRANCH_W ** -0.5)
    w_out = nrm(26, (DEPTH, D_MODEL, D_MODEL), D_MODEL ** -0.5)
    return {'x_prompt': x_prompt, 'x_sample': x_sample, 'cache_k': cache_k, 'cache_v': cache_v,
            'cache_logf': cache_logf, 'state_C': state_C, 'state_n': state_n, 'state_m': state_m,
            'page_table': page_table, 'c_prompt': c_prompt, 'c_sample': c_sample,
            'w_ada': w_ada, 'b_ada': b_ada, 'g_norm': g_norm, 'w_ff_up': w_ff_up, 'w_ff_down': w_ff_down,
            'w_in': w_in, 'g_va': g_va, 'w_s': w_s, 'b_s': b_s, 'g_qb': g_qb, 'g_kb': g_kb,
            'b_fb': b_fb, 'b_ic': b_ic, 'b_fc': b_fc, 'w_branch': w_branch, 'w_out': w_out}

def reference(x_prompt, x_sample, cache_k, cache_v, cache_logf, state_C, state_n, state_m, page_table,
              c_prompt, c_sample, w_ada, b_ada, g_norm, w_ff_up, w_ff_down, w_in, g_va, w_s, b_s,
              g_qb, g_kb, b_fb, b_ic, b_fc, w_branch, w_out):
    xp, xs = x_prompt, x_sample
    st_p, st_s, chunk_v = [], [], []
    for l in range(DEPTH):
        lw = (w_ada[l], b_ada[l], g_norm[l], w_ff_up[l], w_ff_down[l], w_in[l], g_va[l], w_s[l], b_s[l],
              g_qb[l], g_kb[l], b_fb[l], b_ic[l], b_fc[l], w_branch[l], w_out[l])
        xp, _, sp = trunk_layer(xp, c_prompt, lw, prompt_mix)
        mix_s = functools.partial(sample_mix, layer=l, cache_k=cache_k, cache_v=cache_v, cache_logf=cache_logf,
                                  page_table=page_table, state_C=state_C, state_n=state_n, state_m=state_m)
        xs, va_s, ss = trunk_layer(xs, c_sample, lw, mix_s)
        st_p.append(sp)
        st_s.append(ss)
        chunk_v.append(va_s)

    def stk(states, i):
        return jnp.stack([s[i] for s in states])

    return (xp, xs,
            stk(st_p, 0), stk(st_p, 1), stk(st_p, 2), stk(st_p, 3), stk(st_p, 4), stk(st_p, 5),
            stk(st_s, 0), stk(st_s, 1), stk(st_s, 2), stk(st_s, 3), stk(st_s, 4), stk(st_s, 5),
            jnp.stack(chunk_v))


_drawn_inputs = setup_inputs


def setup_inputs(seed=0):
    import zlib

    import numpy as np

    out = dict(_drawn_inputs(seed))
    spreads = {}
    factors = {'cache_logf': 5.575, 'g_qb': 8.0}
    for name, (base, spread) in spreads.items():
        noise = np.random.default_rng([zlib.crc32(name.encode()), seed]).standard_normal(out[name].shape)
        drawn = base * np.exp(spread * noise) if base else spread * noise
        out[name] = jnp.asarray(drawn.astype(out[name].dtype))
    for name, factor in factors.items():
        out[name] = (out[name] * factor).astype(out[name].dtype)
    return out
```

```python
from contextlib import ExitStack, contextmanager

import numpy as np

import concourse.bass as bass
from concourse import mybir

F32 = mybir.dt.float32
I32 = mybir.dt.int32
ACT = mybir.ActivationFunctionType
ALU = mybir.AluOpType
AX = mybir.AxisListType

P = 128
L = 2
D = 1024
KD = D // P
NP = 512
SEQS, STEPS = 8, 4
NS = SEQS * STEPS
T = NP + NS
HALF = T // 2
TILES = NP // P
C = 1 + SEQS
FF = 2816
KF = FF // P
PAGES, PAGE = 8, 128
PAST = PAGES * PAGE
POOL = 80
HB, DB = 8, 64
HC, DKC, DVC = 4, 64, 128
ROWS = HB + HC
BIG = 1.0e30
EPS = 1e-6
SLOT = 4096
AREA = 29280
ADA_STEPS, UP_STEPS, DOWN_STEPS, OUT_STEPS = 18, 11, 8, 2

_CONSTS = dict(ident=P, ones=P, halfones=P, later=P, earlier=P, tril01=P, sel_neg=ROWS * P, sel_pair=2 * P,
               seq_later=NS, seq01=NS, own_seq=SEQS, new_mask=2 * NS, new_seq=2 * 4)
CONST_AT, _n = {}, 0
for _k, _w in _CONSTS.items():
    CONST_AT[_k] = (_n, _w)
    _n += _w
CONST_W = _n


def constants():
    c = np.zeros((P, CONST_W), np.float32)

    def put(name, a):
        at, w = CONST_AT[name]
        a = a.reshape(a.shape[0], -1)
        assert a.shape[1] == w
        c[:a.shape[0], at:at + w] = a

    i = np.arange(P)
    put("ident", np.eye(P))
    put("ones", np.ones((P, P)))
    put("halfones", (i[:, None] // 64 == i[None] // 64) * 1.0)
    put("later", np.where(i[None] >= i[:, None], 0, -BIG))
    put("earlier", np.where(i[None] <= i[:, None], 0, -BIG))
    put("tril01", (i[None] >= i[:, None]) * 1.0)
    sel = np.zeros((ROWS, ROWS, P))
    for r in range(ROWS):
        sel[r, r] = -1 if r >= HB else 1
    put("sel_neg", sel)
    pair = np.zeros((ROWS, 2, P))
    for h in range(HC):
        pair[HB + h, h // 2, 64 * (h % 2):64 * (h % 2) + 64] = 1
    put("sel_pair", pair)
    t = np.arange(NS)
    same = t[:, None] // STEPS == t[None] // STEPS
    put("seq_later", np.where(same & (t[None] >= t[:, None]), 0, -BIG))
    put("seq01", (same & (t[None] >= t[:, None])) * 1.0)
    put("own_seq", (t[:, None] // STEPS == np.arange(SEQS)[None]) * 1.0)
    new = np.full((P, 2, NS), -BIG)
    for g in range(2):
        own = (t[None] // STEPS == 4 * g + i[:, None] // 32) & (t[None] % STEPS <= i[:, None] % STEPS)
        new[:, g][own] = 0
    put("new_mask", new)
    put("new_seq", (t[:, None] // STEPS == np.arange(8)[None]) * 1.0)
    return c


class Tally:

    def __init__(self, sem, unit=1, seed=0):
        self.sem, self.unit, self.n, self.loops = sem, unit, seed, []

    def value(self, ahead=0):
        v = (self.n + ahead) * self.unit
        for reg, stride in self.loops:
            v = reg * (stride * self.unit) + v
        return v


@contextmanager
def repeat(eng, count, strides):
    before = {t: t.n for t in strides}
    with eng.Fori(0, count) as i:
        for t, s in strides.items():
            t.loops.append((i, s))
        yield i
        for t, s in strides.items():
            assert t.n - before[t] == s, (str(t.sem), t.n - before[t], s)
            t.loops.pop()
            t.n += s * (count - 1)


UA, VA, QKC, VC, OC, QB, KB, VB = range(8)

VE_LINKS = 192

UNITS = dict(ada=ADA_STEPS, norm=1, up=4 * UP_STEPS, down=DOWN_STEPS,
             gate=4 + 5 + 4, mlstm_in=4 + 5 + 4 + 1 + 5 + 1 + 4 + 1, mlstm=2 * HC + 1 + 2 + 1,
             fox_in=4 + 4 + 5 + 8, fox=HB + HB // 2, fox_sample=2 * 3, merge=6 * KD, out=KD)
UNITS_L = sum(UNITS[k] for k in UNITS) + 2 + UNITS["up"] + UNITS["down"]
STEPS_L = ADA_STEPS + 2 * (UP_STEPS + DOWN_STEPS) + 8 + 2 * KD + OUT_STEPS


def build(nc, d, out):
    ctx = ExitStack()
    with ctx:
        def sb(name, shape, dt=F32):
            return ctx.enter_context(nc.sbuf_tensor(name, shape, dt))

        def sem(name):
            return ctx.enter_context(nc.semaphore(name))

        cst = sb("cst", [P, CONST_W])
        W = [sb(f"w{i}", [P, SLOT]) for i in range(2)]
        X = sb("x", [P, KD, T])
        H = sb("h", [P, KD, T])
        MOD = sb("mod", [P, 9 * KD, C])
        AMP = sb("amp", [P, 3, KD, C])
        COND = sb("cond", [P, KD, C])
        BADA = sb("bada", [P, 9 * KD])
        GN = sb("gn", [P, 3, KD])
        GVA = sb("gva", [P, 512])
        BS = sb("bs", [P, 4, P])
        WST = sb("wst", [P, 4, P])
        WSS = sb("wss", [NS, 4, NS])
        BROWS = sb("brows", [44, 1])
        GQK = sb("gqk", [P, 2])
        WFI = sb("wfi", [P, KD, 44])
        M0 = sb("m0", [ROWS, SEQS])
        N0 = sb("n0", [P, 2, SEQS])
        TABLE = sb("table", [1, SEQS * PAGES], I32)
        EPSC = sb("epsc", [P, 2])
        ZERO = sb("zero", [P, 1])
        QS = sb("qs", [P, 4, SEQS, HB, STEPS])
        QW = sb("qw", [P, 2, 2, NS])
        area = sb("area", [P, AREA])
        at = [0]

        def take(*shape, start=None):
            n = int(np.prod(shape))
            o = at[0] if start is None else start
            if start is None:
                at[0] += n
                assert at[0] <= AREA, at[0]
            v = area[:, o:o + n]
            names = "abcd"[:len(shape)]
            if len(shape) > 1:
                v = v.rearrange(f"p ({' '.join(names)}) -> p {' '.join(names)}",
                                **{k: s for k, s in zip(names[1:], shape[1:])})
            return v, o

        YS, _ = take(3, 4, T)
        YA, YB, YC = YS[:, 0], YS[:, 1], YS[:, 2]
        QKB, o_qk = take(8, T)
        QKC_, _ = take(4, T, start=o_qk + 4 * T)
        ROWG, _ = take(T, start=o_qk)
        ROWM, _ = take(T, start=o_qk + T)
        SROW, _ = take(3, NS, start=o_qk + 2 * T)
        MT, _ = take(KD, T, start=o_qk)
        TV, o_tv = take(5, 512)
        CS, _ = take(2, SEQS, P, start=o_tv)
        TV2, _ = take(5, 512)
        ROWA, _ = take(T)
        ROWF, _ = take(T)
        COL, _ = take(84)
        KCT, o_k = take(5, 256)
        EM, _ = take(2, 512)
        NF, _ = take(4, 512, start=o_k)
        GB, o_g = take(4, T)
        FB, _ = take(PAST + NS, start=o_g)
        LFR, _ = take(PAST, start=o_g + PAST + NS)
        SCR, o_s = take(8, 512)
        SSC, _ = take(PAST + NS, start=o_s)
        PT, _ = take(9, P, start=o_s + PAST + NS)
        RS, _ = take(T, start=o_s)
        RT, _ = take(2, T, start=o_s)
        SQ, _ = take(2, T, start=o_s + 2 * T)
        GT, _ = take(3, T, start=o_s)
        ZT, _ = take(2, T, start=o_s + 3 * T)
        VBLK, _ = take(2, SEQS, P, start=o_s)
        PG, _ = take(4, 512)
        EMS, _ = take(4, NS)
        WIB, _ = take(2, NS)
        QN, _ = take(2, 2, NS)
        ARG, _ = take(4, NS)
        ES, _ = take(4, NS)
        WSM, _ = take(4, NS)
        WKC, _ = take(4, TILES)
        DIAG, _ = take(2, P)
        SMALL, _ = take(32)
        TMP, _ = take(2, NS)
        ACTS, _ = take(KF, T, start=0)

        G = ctx.enter_context(nc.psum_tensor("g", [P, 4, 512], F32))
        Q = ctx.enter_context(nc.psum_tensor("q", [P, 2, 512], F32))
        TB = ctx.enter_context(nc.psum_tensor("tb", [P, 2, 512], F32))

        def const(name, rows=P):
            a, w = CONST_AT[name]
            return cst[0:rows, a:a + w]

        ident, ones, halfones = const("ident"), const("ones"), const("halfones")
        later, earlier, tril01 = const("later"), const("earlier"), const("tril01")
        sel_neg = const("sel_neg", ROWS).rearrange("p (r n) -> p r n", n=P)
        sel_pair = const("sel_pair", ROWS).rearrange("p (r n) -> p r n", n=P)
        seq_later, seq01, own_seq = const("seq_later", NS), const("seq01", NS), const("own_seq", NS)
        new_mask = const("new_mask").rearrange("p (g n) -> p g n", g=2)
        new_seq = const("new_seq", NS)

        s_in = sem("inputs_in")
        s_eps = sem("eps_set")
        s_zero = sem("spread_zeroed")
        s_cond = sem("cond_silu")
        s_unit = sem("unit_done")
        s_dr = [sem("drained0"), sem("drained1")]
        s_w = [sem("weights_in0"), sem("weights_in1")]
        s_wu = [sem("weights_used0"), sem("weights_used1")]
        s_small = sem("small_in")
        s_smallf = sem("small_used")
        s_sq = sem("squares")
        s_rms = sem("root_ms")
        s_h = sem("h_ready")
        s_mods = sem("mods_ready")
        s_vrms = sem("va_rms")
        s_vardy = sem("va_ready")
        s_chunkv = sem("chunk_v_out")
        s_ws = sem("w_s_masked")
        s_x1 = sem("gate_rows")
        s_sp = sem("softplus_rows")
        s_rowd = sem("row_diff")
        s_rows = sem("rows_ready")
        s_wrow = sem("weight_rows")
        s_exr = sem("exp_rows")
        s_qk = sem("mlstm_scores")
        s_diag = sem("diag_ready")
        s_e = sem("decay_ready")
        s_wt = sem("mlstm_weights")
        s_yc = sem("yc_head")
        s_wkc = sem("key_weights")
        s_kw = sem("weighted_keys")
        s_sintra = sem("sample_scores")
        s_sarg = sem("sample_args")
        s_ses = sem("sample_decay")
        s_sw = sem("sample_weights")
        s_c0 = sem("state_in")
        s_c0f = sem("state_free")
        s_num = sem("sample_num")
        s_vblk = sem("v_spread")
        s_kws = sem("sample_weighted_keys")
        s_st = sem("state_out")
        s_stn = sem("state_new")
        s_sqn = sem("qk_squares")
        s_rtn = sem("qk_root")
        s_qkr = sem("qk_ready")
        s_sc = sem("fox_scores")
        s_nf = sem("fox_bias")
        s_max = sem("fox_max")
        s_exp = sem("fox_exp")
        s_p = sem("fox_probs")
        s_pt = sem("fox_turned")
        s_ptc = sem("fox_turned_copied")
        s_hpd = sem("fox_pair_done")
        s_lf = sem("past_logf_in")
        s_lff = sem("past_logf_used")
        s_pg = [sem(f"page_in{i}") for i in range(4)]
        s_pgu = sem("pages_used")
        s_qs = sem("queries_spread")
        s_ln = sem("new_logf_spread")
        s_ss = sem("sample_fox_scores")
        s_smx = sem("sample_fox_max")
        s_sex = sem("sample_fox_exp")
        s_ps = sem("sample_fox_probs")
        s_pv = sem("sample_fox_out")
        s_pvc = sem("sample_fox_kept")
        s_xup = sem("x_updated")
        s_gt = sem("merge_gates")
        s_m = sem("merged")
        s_out = sem("outputs_out")
        s_outa = sem("outputs_out_act")
        s_dv = sem("vector_step")
        s_ac = sem("scalar_step")
        s_pl = sem("pool_step")
        s_ada = sem("ada_bias_added")

        s_apart = sem("wait_apart")

        block = ctx.enter_context(nc.Block())

        def apart(eng):
            eng.sem_inc(s_apart, 1)

        class Units:

            def __init__(self):
                self.u, self.d, self.k = Tally(s_unit), [Tally(s_dr[0], seed=1), Tally(s_dr[1], seed=1)], 0

            def take(self, n=1):
                for _ in range(n):
                    p = self.k % 2
                    self.k += 1
                    self.u.n += 1
                    self.d[p].n += 1
                return p

            def layer(self):
                assert UNITS_L % 2 == 0, UNITS_L
                return self.strides(UNITS_L)

            def strides(self, n):
                assert n % 2 == 0
                return {self.u: n, self.d[0]: n // 2, self.d[1]: n // 2}

        def halves(x):
            return x.rearrange("p (a n) -> p a n", a=2)

        @block.sync
        def _(sp):
            sp.dma_start(cst[:], d["consts"]).then_inc(s_in, 16)
            sp.dma_start(COND[:], d["c"]).then_inc(s_in, 16)
            sp.dma_start(X[:], d["x"]).then_inc(s_in, 16)
            used = [Tally(s_wu[0]), Tally(s_wu[1])]
            landed = [Tally(s_w[0], 16), Tally(s_w[1], 16)]
            k = [0]

            def load(src, n):
                s = k[0] % 2
                k[0] += 1
                used[s].n += 1
                sp.wait_ge(s_wu[s], used[s].value())
                sp.dma_start(W[s][:, 0:n], src.rearrange("a p n -> (a p) n")).then_inc(s_w[s], 16)

            def stream(name, n_steps, size, base):
                with repeat(sp, n_steps // 2, {used[0]: 1, used[1]: 1}) as i:
                    for j in range(2):
                        load(d[name][bass.ds(base + i * 2 + j, 1)], size)
                if n_steps % 2:
                    load(d[name][bass.ds(base + n_steps - 1, 1)], size)

            with repeat(sp, L, {used[0]: STEPS_L // 2, used[1]: STEPS_L // 2}) as l:
                stream("w_ada", ADA_STEPS, SLOT, l * ADA_STEPS)
                for f in range(2):
                    if f == 1:
                        for n in range(8):
                            load(d["w_in"][bass.ds(l * 8 + n, 1)], SLOT)
                        with repeat(sp, KD, {used[0]: 1, used[1]: 1}) as m:
                            load(d["w_gate"][bass.ds(l * KD + m, 1)], KD * 3 * P)
                            load(d["w_branch"][bass.ds(l * KD + m, 1)], 12 * P)
                        stream("w_out", OUT_STEPS, SLOT, l * OUT_STEPS)
                    stream("w_up", UP_STEPS, SLOT, (l * 2 + f) * UP_STEPS)
                    stream("w_down", DOWN_STEPS, KF * P, (l * 2 + f) * DOWN_STEPS)
            sp.wait_ge(s_xup, KD + L * 3 * KD)
            sp.dma_start(out["y"], X[:]).then_inc(s_out, 16)
            sp.wait_ge(s_out, 16)

        @block.gpsimd
        def _(po):
            po.dma_start(TABLE[:], d["page_table"]).then_inc(s_pl, 16)
            po.wait_ge(s_pl, 16)
            small_free = Tally(s_smallf)
            lf_free = Tally(s_lff)
            pages = Tally(s_pgu)
            c0f = Tally(s_c0f)
            with repeat(po, L, {small_free: 1, lf_free: 2, pages: 4 * SEQS * PAGES // 2, c0f: 1}) as l:
                small_free.n += 1
                po.wait_ge(s_smallf, small_free.value())
                for dst, name in ((BADA[:], "b_ada"), (GN[:], "g_norm"), (GVA[:], "g_va"), (BS[:], "b_s"),
                                  (WST[:], "w_s"), (WSS[:], "w_s_new"), (BROWS[:], "b_rows"), (GQK[:], "g_qk"),
                                  (WFI[:], "w_rows"), (M0[:], "m0"), (N0[:], "n0")):
                    src = d[name][bass.ds(l, 1)]
                    if name == "g_va":
                        src = src.rearrange("a n -> (a n)")[None, :].to_broadcast([P, 512])
                    elif name == "b_s":
                        src = src.rearrange("a g n -> (a g) n")[None, :, :].to_broadcast([P, 4, P])
                    elif len(src.shape) == 3:
                        src = src.rearrange("a p n -> (a p) n")
                    else:
                        src = src.rearrange("a p g n -> (a p) g n")
                    po.dma_start(dst, src).then_inc(s_small, 16)
                c0f.n += 1
                po.wait_ge(s_c0f, c0f.value())
                po.dma_start(CS, d["C0"][bass.ds(l, 1)].rearrange("a p h s v -> (a p) h s v")).then_inc(s_c0, 16)
                for g in range(2):
                    lf_free.n += 1
                    po.wait_ge(s_lff, lf_free.value())
                    apart(po)
                    for s in range(4):
                        with po.Fori(0, PAGES) as pg:
                            r = po.value_load(TABLE[0:1, bass.ds(pg + (g * 4 + s) * PAGES, 1)], min_val=0,
                                              max_val=POOL - 1)
                            src = d["cache_f"][bass.ds(l * POOL + r, 1)].rearrange("a h n -> (a h) n")
                            po.dma_start(LFR[32 * s:32 * s + 32, bass.ds(pg * PAGE, PAGE)],
                                         src[:, None, :].to_broadcast([HB, STEPS, PAGE])).then_inc(s_lf, 16)
                    for cache in ("cache_k", "cache_v"):
                        with repeat(po, 8, {pages: 4}) as i:
                            for slot in range(4):
                                r = po.value_load(TABLE[0:1, bass.ds(i * 4 + (g * 32 + slot), 1)], min_val=0,
                                                  max_val=POOL - 1)
                                pages.n += 1
                                po.wait_ge(s_pgu, pages.value())
                                po.dma_start(PG[:, slot, :], d[cache][bass.ds(l * POOL + r, 1)]
                                             .rearrange("a p n -> (a p) n")).then_inc(s_pg[slot], 16)

        @block.tensor
        def _(pe):
            un = Units()
            w_in = [Tally(s_w[0], 16), Tally(s_w[1], 16)]
            hr = Tally(s_h)
            sq = Tally(s_sq)
            small = Tally(s_small, 16)
            t = {k: Tally(s) for k, s in dict(vardy=s_vardy, ws=s_ws, rows=s_rows, wrow=s_exr, e=s_wt, kw=s_kw,
                                               sw=s_sw, vblk=s_vblk, kws=s_kws, sqn=s_sqn, qkr=s_qkr, mx=s_max,
                                               p=s_p, ptc=s_ptc, qs=s_qs, ln=s_ln, ps=s_ps, smx=s_smx, pvc=s_pvc,
                                               m=s_m).items()}
            c0 = Tally(s_c0, 16)
            pin = [Tally(s_pg[i], 16) for i in range(4)]
            step, pend = [0], [1]

            def wait(tally, n=1):
                tally.n += n
                pe.wait_ge(tally.sem, tally.value())

            def mm(o, a, b, start, stop, **kw):
                ins = pe.matmul(o, a, b, start=start, stop=stop, skip_group_check=True, **kw)
                if pend[0] is not None:
                    ins.then_inc(s_wu[pend[0]], 1)
                    pend[0] = None
                return ins

            def turn(o, a, idn):
                return pe.transpose(o, a, idn)

            def unit():
                p = un.k % 2
                pe.wait_ge(s_dr[p], un.d[p].value())
                un.take()
                return p

            def weights():
                s = step[0] % 2
                step[0] += 1
                wait(w_in[s])
                return s

            def left(s):
                pend[0] = s

            def product(p, blocks, rhs, m=P, first=None):
                n = len(blocks)
                for k in range(n):
                    if first is not None:
                        wait(first)
                    for h in range(2):
                        last = mm(G[0:m, 2 * p + h, 0:HALF], blocks[k], rhs(k)[:, h * HALF:(h + 1) * HALF],
                                  k == 0, k == n - 1)
                last.then_inc(s_unit, 1)

            def norm_sums():
                p = unit()
                product(p, [ones] * KD, lambda k: H[:, k, :], first=sq)

            def hk(k):
                return H[:, k, :]

            def up():
                def one(first):
                    s = weights()
                    w = W[s][:, :].rearrange("p (k n) -> p k n", k=KD)
                    for j in range(2):
                        for ab in range(2):
                            c = ab * 256 + j * P
                            product(unit(), [w[:, k, c:c + P] for k in range(KD)], hk,
                                    first=hr if first and j + ab == 0 else None)
                    left(s)
                one(True)
                one(False)
                with repeat(pe, UP_STEPS // 2 - 1, un.strides(8) | {w_in[0]: 1, w_in[1]: 1}):
                    one(False)
                    one(False)
                one(False)

            def down():
                for q in range(2):
                    pe.wait_ge(s_dr[q], un.d[q].value())
                apart(pe)
                with repeat(pe, DOWN_STEPS // 2, un.strides(2) | {w_in[0]: 1, w_in[1]: 1}):
                    for _ in range(2):
                        s = weights()
                        product(unit(), [W[s][:, k * P:(k + 1) * P] for k in range(KF)], lambda k: ACTS[:, k, :])
                        left(s)

            def project(blocks, first=None):
                s = weights()
                w = W[s][:, :].rearrange("p (k n) -> p k n", k=KD)
                for b in range(blocks):
                    product(unit(), [w[:, k, b * P:(b + 1) * P] for k in range(KD)], hk,
                            first=first if b == 0 else None)
                left(s)

            def project_tokens():
                s = weights()
                for i in range(5):
                    p, m = unit(), P if i < TILES else NS
                    for k in range(KD):
                        last = mm(G[0:m, 2 * p, :], H[:, k, i * P:i * P + m], W[s][:, k * 512:(k + 1) * 512],
                                  k == 0, k == KD - 1)
                    last.then_inc(s_unit, 1)
                left(s)

            pe.wait_ge(s_in, 48)
            strides = un.layer() | {w_in[0]: STEPS_L // 2, w_in[1]: STEPS_L // 2, hr: 3 * KD, sq: 3 * KD, small: 11,
                                    t["vardy"]: 5, t["ws"]: 2, t["rows"]: 1, t["wrow"]: 1, t["e"]: 16, t["kw"]: 1,
                                    t["sw"]: 1, t["vblk"]: 4, t["kws"]: 1, t["sqn"]: 8, t["qkr"]: 8, t["mx"]: 32,
                                    t["p"]: 32, t["ptc"]: 32, t["qs"]: 1, t["ln"]: 2, t["ps"]: 2, t["smx"]: 2,
                                    t["pvc"]: 2, t["m"]: KD, c0: 1}
            strides |= {q: 32 for q in pin}
            pe.wait_ge(s_cond, 1)
            with repeat(pe, L, strides):
                with repeat(pe, ADA_STEPS // 2, un.strides(2) | {w_in[0]: 1, w_in[1]: 1}):
                    for _ in range(2):
                        s, p = weights(), unit()
                        w = W[s][:, :].rearrange("p (k n) -> p k n", k=KD)
                        for b in range(4):
                            for k in range(KD):
                                last = mm(G[:, 2 * p, b * C:(b + 1) * C], w[:, k, b * P:(b + 1) * P], COND[:, k, :],
                                          k == 0, k == KD - 1)
                        last.then_inc(s_unit, 1)
                        left(s)
                norm_sums()
                up()
                down()
                norm_sums()
                project(4, first=hr)
                project_tokens()
                wait(small, 11)
                wait(t["ws"], 2)
                wait(t["vardy"], 5)
                for g in range(4):
                    p = unit()
                    for n in range(TILES):
                        mm(G[:, 2 * p, n * P:(n + 1) * P], TV[:, n, g * P:(g + 1) * P], WST[:, g, :], True, True)
                    mm(G[:, 2 * p + 1, 0:NS], TV[0:NS, TILES, g * P:(g + 1) * P], WSS[:, g, :], True, True)\
                        .then_inc(s_unit, 1)
                project(4)
                project_tokens()
                project(4)
                p = unit()
                product(p, [WFI[:, k, :] for k in range(KD)], hk, m=44)
                for i in range(5):
                    p, m = unit(), P if i < TILES else NS
                    for hp in range(2):
                        last = turn(G[0:m, 2 * p, hp * P:(hp + 1) * P], QKC_[:, 2 + hp, i * P:i * P + m], ident)
                    last.then_inc(s_unit, 1)
                wait(t["rows"])
                wait(t["wrow"])
                p = unit()
                apart(pe)
                for i in range(5):
                    m = P if i < TILES else NS
                    turn(G[0:m, 2 * p, i * 12:i * 12 + 12], ROWA[0:ROWS, i * P:i * P + m], ident[0:ROWS, 0:ROWS])
                turn(G[0:NS, 2 * p, 60:72], SROW[0:ROWS, 1, :], ident[0:ROWS, 0:ROWS])
                turn(G[0:NS, 2 * p, 72:84], ROWF[0:ROWS, NP:T], ident[0:ROWS, 0:ROWS]).then_inc(s_unit, 1)
                for h in range(HC):
                    product(unit(), [sel_neg[:, HB + h, :]], lambda k: ROWG[0:ROWS, :])
                p = unit()
                for hp in range(2):
                    last = mm(G[:, 2 * p, hp * NS:(hp + 1) * NS], sel_pair[:, hp, :], SROW[0:ROWS, 0, :], True, True)
                last.then_inc(s_unit, 1)
                items = [(h, j) for h in range(HC) for j in range(TILES)]
                pair = [None]

                def qk(n):
                    h, j = items[n]
                    r = slice(64 * (h % 2), 64 * (h % 2) + 64)
                    mm(Q[:, n % 2, j * P:NP], QKC_[r, 2 + h // 2, j * P:(j + 1) * P], QKC_[r, h // 2, j * P:NP],
                       True, True).then_inc(s_qk, 1)

                def weigh(n):
                    h, j = items[n]
                    wait(t["e"])
                    if j == 0:
                        pair[0] = unit()
                    p, w = pair[0], SCR[:, 2 + n % 2, j * P:NP]
                    mm(G[:, 2 * p, j * P:NP], TV2[:, j, h * P:(h + 1) * P], w, j == 0, j == TILES - 1)
                    last = mm(G[:, 2 * p + 1, j * P:NP], ones, w, j == 0, j == TILES - 1)
                    if j == TILES - 1:
                        last.then_inc(s_unit, 1)

                for h in range(HC):
                    for j in range(TILES):
                        n = h * TILES + j
                        if n == 0:
                            product(unit(), [sel_neg[:, HB, :]], lambda k: ROWM[0:ROWS, :])
                            qk(0)
                        if n + 1 < len(items):
                            qk(n + 1)
                        weigh(n)
                        if j == TILES - 1 and h + 1 < HC:
                            product(unit(), [sel_neg[:, HB + h + 1, :]], lambda k: ROWM[0:ROWS, :])
                wait(t["kw"])
                p = unit()
                for h in range(HC):
                    r = slice(64 * (h % 2), 64 * (h % 2) + 64)
                    for j in range(TILES):
                        mm(G[r, 2 * p, (h // 2) * P:(h // 2 + 1) * P], KCT[:, j, h * 64:(h + 1) * 64],
                           TV2[:, j, h * P:(h + 1) * P], j == 0, j == TILES - 1)
                for hp in range(2):
                    for j in range(TILES):
                        last = mm(G[:, 2 * p + 1, hp:hp + 1], KCT[:, j, hp * P:(hp + 1) * P], ones[:, 0:1],
                                  j == 0, j == TILES - 1)
                last.then_inc(s_unit, 1)
                for h in range(HC):
                    r = slice(64 * (h % 2), 64 * (h % 2) + 64)
                    last = mm(Q[0:NS, h % 2, (h // 2) * NS:(h // 2 + 1) * NS], QKC_[r, 2 + h // 2, NP:T],
                              QKC_[r, h // 2, NP:T], True, True)
                last.then_inc(s_sintra, 1)
                wait(t["sw"])
                wait(c0)
                for h in range(HC):
                    mm(TB[:, 0, h * NS:(h + 1) * NS], TV2[0:NS, TILES, h * P:(h + 1) * P], WSM[0:NS, h, :],
                       h == 0, False)
                mm(TB[:, 1, 0:HC * NS], ones[0:NS, :], WSM[0:NS, :, :], True, False)
                mm(TB[:, 1, 0:HC * NS], ones, QN, False, True)
                for hp in range(2):
                    for s in range(SEQS):
                        o = TB[:, 0, 2 * hp * NS:2 * (hp + 1) * NS].rearrange("p (h n) -> p h n", h=2)
                        last = mm(o[:, :, s * STEPS:(s + 1) * STEPS], CS[:, hp, s, :],
                                  QW[:, hp, :, s * STEPS:(s + 1) * STEPS], False, hp == 1 and s == SEQS - 1)
                last.then_inc(s_num, 1)
                wait(t["kws"])
                for hp in range(2):
                    p = unit()
                    for h2 in range(2):
                        wait(t["vblk"])
                        h = 2 * hp + h2
                        for sh in range(2):
                            last = mm(G[64 * h2:64 * h2 + 64, 2 * p + sh, :], KCT[0:NS, TILES, h * 64:(h + 1) * 64],
                                      VBLK[0:NS, h2, 4 * sh:4 * sh + 4, :], True, True)
                    last.then_inc(s_unit, 1)
                p = unit()
                for hp in range(2):
                    last = mm(G[:, 2 * p, hp * SEQS:(hp + 1) * SEQS], KCT[0:NS, TILES, hp * P:(hp + 1) * P], own_seq,
                              True, True)
                last.then_inc(s_unit, 1)
                project(4)
                project(4)
                project_tokens()
                last_slot, pend[0] = pend[0], None
                for m in range(8):
                    wait(t["sqn"])
                    product(unit(), [halfones], lambda k: SQ[:, m % 2, :])
                wait(t["qkr"], 8)
                for hp in range(4):
                    for h in (2 * hp, 2 * hp + 1):
                        product(unit(), [sel_neg[:, h, :]], lambda k: ROWA[0:ROWS, :])
                    pair = unit()
                    todo = [(h, i) for h in (2 * hp, 2 * hp + 1) for i in range(TILES)]

                    def scores(n):
                        h, i = todo[n]
                        r = slice(64 * (h % 2), 64 * (h % 2) + 64)
                        it = hp * 8 + n
                        if it >= 2:
                            wait(t["mx"])
                        mm(Q[:, it % 2, 0:(i + 1) * P], QKB[r, hp, i * P:(i + 1) * P], QKB[r, 4 + hp, 0:(i + 1) * P],
                           True, False)
                        mm(Q[:, it % 2, i * P:(i + 1) * P], ident, earlier, False, True).then_inc(s_sc, 1)

                    def turns(n):
                        h, i = todo[n]
                        it = hp * 8 + n
                        wait(t["p"])
                        for j in range(i + 1):
                            last = turn(TB[:, it % 2, j * P:(j + 1) * P], SCR[:, it % 2, j * P:(j + 1) * P], ident)
                        last.then_inc(s_pt, 1)

                    def values(n):
                        h, i = todo[n]
                        it = hp * 8 + n
                        wait(t["ptc"])
                        r = slice(64 * (h % 2), 64 * (h % 2) + 64)
                        for j in range(i + 1):
                            last = mm(G[r, 2 * pair, i * P:(i + 1) * P], TV2[:, j, h * 64:(h + 1) * 64],
                                      SCR[:, 2 + it % 2, j * P:(j + 1) * P], j == 0, j == i)
                        if n == 7:
                            last.then_inc(s_unit, 1)

                    for n in range(8 + 2):
                        if n < 8:
                            scores(n)
                        if 1 <= n <= 8:
                            turns(n - 1)
                        if n >= 2:
                            values(n - 2)
                wait(t["mx"], 2)
                wait(t["qs"])
                for g in range(2):
                    wait(t["ln"])
                    p = unit()
                    mm(G[:, 2 * p, 0:NS], DIAG[0:NS, g, :], seq01, True, True).then_inc(s_unit, 1)
                    for s in range(4):
                        r = slice(32 * s, 32 * s + 32)
                        for pg in range(PAGES):
                            wait(pin[pg % 4])
                            for hp in range(4):
                                last = mm(Q[r, pg // 4, (pg % 4) * P:(pg % 4 + 1) * P],
                                          QS[:, hp, 4 * g + s, :, :], PG[:, pg % 4, hp * P:(hp + 1) * P],
                                          hp == 0, hp == 3)
                            last.then_inc(s_pgu, 1)
                        for hp in range(4):
                            last = mm(TB[r, 0, 0:NS], QS[:, hp, 4 * g + s, :, :], QKB[:, 4 + hp, NP:T],
                                      hp == 0, hp == 3)
                    last.then_inc(s_ss, 1)
                    wait(t["ps"])
                    p = unit()
                    for pg in range(PAGES):
                        last = turn(G[:, 2 * p + pg // 4, (pg % 4) * P:(pg % 4 + 1) * P],
                                    SSC[:, pg * P:(pg + 1) * P], ident)
                    last.then_inc(s_unit, 1)
                    p = unit()
                    apart(pe)
                    turn(G[0:NS, 2 * p, 0:P], SSC[:, PAST:PAST + NS], ident).then_inc(s_unit, 1)
                    for q in range(2):
                        pe.wait_ge(s_dr[q], un.d[q].value())
                    for s in range(4):
                        for pg in range(PAGES):
                            wait(pin[pg % 4])
                            for hp in range(4):
                                last = mm(TB[:, 1, (s * 4 + hp) * 8:(s * 4 + hp + 1) * 8],
                                          PG[:, pg % 4, hp * P:(hp + 1) * P],
                                          PT[:, pg, s * 32 + hp * 8:s * 32 + hp * 8 + 8],
                                          s + pg + hp == 0, False)
                            last.then_inc(s_pgu, 1)
                    for s in range(4):
                        for hp in range(4):
                            last = mm(TB[:, 1, (s * 4 + hp) * 8:(s * 4 + hp + 1) * 8],
                                      TV2[0:NS, TILES, hp * P:(hp + 1) * P],
                                      PT[0:NS, 8, s * 32 + hp * 8:s * 32 + hp * 8 + 8], False, s + hp == 6)
                    last.then_inc(s_pv, 1)
                    wait(t["pvc"])
                    wait(t["smx"])
                pend[0] = last_slot
                apart(pe)
                with repeat(pe, KD, un.strides(6) | {w_in[0]: 1, w_in[1]: 1}):
                    s = weights()
                    for b in range(3):
                        product(unit(), [W[s][:, (k * 3 + b) * P:(k * 3 + b + 1) * P] for k in range(KD)], hk)
                    left(s)
                    s = weights()
                    for b in range(3):
                        product(unit(), [W[s][:, (b * 4 + k) * P:(b * 4 + k + 1) * P] for k in range(4)],
                                lambda k: YS[:, b, k, :])
                    left(s)
                wait(t["m"], KD)
                apart(pe)
                with repeat(pe, OUT_STEPS // 2, un.strides(8) | {w_in[0]: 1, w_in[1]: 1}):
                    for _ in range(2):
                        s = weights()
                        w = W[s][:, :].rearrange("p (k n) -> p k n", k=KD)
                        for b in range(4):
                            product(unit(), [w[:, k, b * P:(b + 1) * P] for k in range(KD)], lambda k: MT[:, k, :])
                        left(s)
                norm_sums()
                up()
                down()

        @block.scalar
        def _(ac):
            un = Units()
            small = Tally(s_small, 16)
            t = {k: Tally(s) for k, s in dict(xup=s_xup, vardy=s_vardy, x1=s_x1, rowd=s_rowd, rows=s_rows,
                                              wrow=s_wrow, diag=s_diag, wt=s_wt, yc=s_yc, sarg=s_sarg, qkr=s_qkr,
                                              mx=s_max, p=s_p, pt=s_pt, smx=s_smx, stn=s_stn).items()}
            st = Tally(s_ac)
            outs = Tally(s_outa, 16)
            outa = d["outs"]

            def wait(tally, n=1):
                tally.n += n
                ac.wait_ge(tally.sem, tally.value())

            def link(ins):
                st.n += 1
                ins.then_inc(s_ac, 1)
                ac.wait_ge(s_ac, st.value())

            def mine():
                p = un.take()
                ac.wait_ge(s_unit, un.u.value())
                return p

            def both(p, m=P):
                return G[0:m, 2 * p:2 * p + 2, 0:HALF]

            def drained(ins, p):
                ins.then_inc(s_dr[p], 1)

            def store(dst, src):
                outs.n += 1
                ac.dma_start(dst, src).then_inc(s_outa, 16)

            def norm():
                for k in range(KD):
                    wait(t["xup"])
                    ac.activation(H[:, k, :], X[:, k, :], ACT.Square).then_inc(s_sq, 1)
                p = mine()
                ac.activation(halves(RS), both(p), ACT.Sqrt, bias=EPSC[:, 0:1], scale=1.0 / D).then_inc(s_rms, 1)

            def up():
                with repeat(ac, KF, un.strides(2)) as m:
                    p = mine()
                    o = ACTS[:, bass.ds(m, 1), :].rearrange("p a (h n) -> p (a h) n", h=2)
                    drained(ac.activation(o, both(p), ACT.Silu, bias=ZERO[:, 0:1]), p)
                    un.take()

            def each(n, f):
                for i in range(n):
                    p = mine()
                    drained(f(i, p), p)

            def tokens(dst, func):
                def f(i, p):
                    m = P if i < TILES else NS
                    return ac.activation(dst[0:m, i, :], G[0:m, 2 * p, :], func, **({} if func == ACT.Copy else
                                                                                  dict(bias=ZERO[0:m, 0:1])))
                each(5, f)

            ac.wait_ge(s_in, 48)
            ac.wait_ge(s_eps, 1)
            ac.activation(COND[:], COND[:], ACT.Silu, bias=ZERO[:, 0:1]).then_inc(s_cond, 1)
            strides = un.layer() | {st: 3, t["xup"]: 24, t["vardy"]: 5, t["x1"]: 1, t["rowd"]: 1, t["rows"]: 1,
                                    t["wrow"]: 1, t["diag"]: 16, t["wt"]: 16, t["yc"]: 5, t["sarg"]: 1,
                                    t["qkr"]: 8, t["mx"]: 32, t["p"]: 32, t["pt"]: 32, t["smx"]: 2, t["stn"]: 4,
                                    outs: 11, small: 11}
            with repeat(ac, L, strides) as l:
                lay = bass.ds(l, 1)
                un.take(ADA_STEPS)
                norm()
                up()
                un.take(DOWN_STEPS)
                norm()
                each(4, lambda i, p: ac.activation(halves(YA[:, i, :]), both(p), ACT.Gelu_apprx_tanh,
                                                   bias=ZERO[:, 0:1]))
                tokens(TV, ACT.Gelu_apprx_tanh)
                for q in range(2):
                    ac.wait_ge(s_dr[q], un.d[q].value())
                for i in range(5):
                    m = P if i < TILES else NS
                    last = ac.activation(SCR[0:m, i, :], TV[0:m, i, :], ACT.Square, accum_out=SMALL[0:m, i:i + 1])
                link(last)
                for i in range(5):
                    m = P if i < TILES else NS
                    ac.activation(SMALL[0:m, 8 + i:9 + i], SMALL[0:m, i:i + 1], ACT.Sqrt, bias=EPSC[0:m, 0:1],
                                  scale=1.0 / 512).then_inc(s_vrms, 1)
                wait(t["vardy"], 5)
                store(outa["chunk_v"][lay].rearrange("a p n -> (a p) n"), TV[0:NS, TILES, :])
                un.take(4)
                each(4, lambda i, p: ac.activation(halves(QKC_[:, i, :]), both(p), ACT.Copy,
                                                   scale=1.0 if i < 2 else DKC ** -0.5))
                tokens(TV2, ACT.Copy)
                each(4, lambda i, p: ac.activation(halves(YC[:, i, :]), both(p), ACT.Sigmoid, bias=ZERO[:, 0:1]))
                un.take()
                wait(t["x1"])
                link(ac.activation(ROWM[0:ROWS], ROWF[0:ROWS], ACT.Abs, bias=ZERO[0:ROWS, 0:1]))
                link(ac.activation(ROWM[0:ROWS], ROWM[0:ROWS], ACT.Exp, bias=ZERO[0:ROWS, 0:1], scale=-1.0))
                ac.activation(ROWM[0:ROWS], ROWM[0:ROWS], ACT.Ln, bias=ones[0:ROWS, 0:1]).then_inc(s_sp, 1)
                wait(t["rowd"])
                store(outa["logf"][lay].rearrange("a h n -> (a h) n"), ROWF[0:HB, :])
                each(5, lambda i, p: ac.activation(KCT[0:P if i < TILES else NS, i, :],
                                                   G[0:P if i < TILES else NS, 2 * p, 0:256], ACT.Copy))
                wait(t["rows"])
                store(outa["m"][lay].rearrange("a h n -> (a h) n"), ROWM[HB:ROWS, NP - 1:T])
                wait(t["wrow"])
                ac.activation(SROW[0:ROWS, 0:2, :], SROW[0:ROWS, 0:2, :], ACT.Exp, bias=ZERO[0:ROWS, 0:1])\
                    .then_inc(s_exr, 1)
                un.take()
                each(4, lambda i, p: ac.activation(halves(GB[:, i, :]), both(p), ACT.Copy))
                un.take()
                for q in range(2):
                    ac.wait_ge(s_dr[q], un.d[q].value())
                for h in range(HC):
                    last = ac.activation(WKC[:, h, :], COL[:, 0:48].rearrange("p (i r) -> p i r", r=12)[:, :, HB + h],
                                         ACT.Exp, bias=GB[:, h, NP - 1:NP])
                last.then_inc(s_wkc, 1)
                for h in range(HC):
                    p = mine()
                    if h >= 2:
                        wait(t["yc"])
                    ac.activation(EM[:, h % 2, 0:HALF], G[:, 2 * p, 0:HALF], ACT.Exp, bias=ZERO[:, 0:1])
                    ac.activation(EM[:, h % 2, HALF:NP], G[:, 2 * p + 1, 0:NP - HALF], ACT.Exp,
                                  bias=ZERO[:, 0:1])
                    drained(ac.activation(EMS[:, h, :], G[:, 2 * p + 1, NP - HALF:HALF], ACT.Exp,
                                          bias=ZERO[:, 0:1]), p)
                    for j in range(TILES):
                        n = h * TILES + j
                        a = COL[:, j * 12 + HB + h:j * 12 + HB + h + 1]
                        wait(t["diag"])
                        if n >= 2:
                            wait(t["wt"])
                        e = SCR[:, n % 2, :]
                        last = ac.activation(e[:, j * P:(j + 1) * P], DIAG[:, n % 2, :], ACT.Exp, bias=a)
                        if j < TILES - 1:
                            last = ac.activation(e[:, (j + 1) * P:NP], GB[:, h, (j + 1) * P:NP], ACT.Exp, bias=a)
                        last.then_inc(s_e, 1)
                    un.take()
                wait(t["wt"], 2)
                wait(t["yc"], 2)
                un.take()
                wait(t["stn"])
                store(outa["C_prompt"][lay].rearrange("a p h v -> (a p) h v"),
                      EM[:, 0, 0:256].rearrange("p (h v) -> p h v", h=2))
                store(outa["n_prompt"][lay].rearrange("a p h -> (a p) h"), EM[:, 1, 0:2])
                wait(t["sarg"])
                for h in range(HC):
                    last = ac.activation(ES[0:NS, h, :], ARG[0:NS, h, :], ACT.Exp,
                                         bias=COL[0:NS, 48 + HB + h:49 + HB + h])
                last.then_inc(s_ses, 1)
                for hp in range(2):
                    un.take()
                    wait(t["stn"])
                    store(outa["C_sample"][lay, hp].rearrange("a p s v -> (a p) s v"), CS[:, hp, :, :])
                un.take()
                wait(t["stn"])
                store(outa["n_sample"][lay].rearrange("a p h s -> (a p) h s"), N0[:])
                wait(t["yc"])
                ac.wait_ge(s_outa, outs.value())
                each(8, lambda i, p: ac.activation(halves(QKB[:, i, :]), both(p), ACT.Copy))
                tokens(TV2, ACT.Copy)
                for q in range(2):
                    ac.wait_ge(s_dr[q], un.d[q].value())
                store(outa["v"][lay, 0:NP].rearrange("a (i p) n -> p (a i) n", p=P), TV2[:, 0:TILES, :])
                store(outa["v"][lay, NP:T].rearrange("a p n -> (a p) n"), TV2[0:NS, TILES, :])
                for m in range(8):
                    ac.activation(SQ[:, m % 2, :], QKB[:, m, :], ACT.Square).then_inc(s_sqn, 1)
                    p = mine()
                    if m >= 2:
                        wait(t["qkr"])
                    ac.activation(halves(RT[:, m % 2, :]), both(p), ACT.Sqrt,
                                  bias=EPSC[:, 1:2] if m < 4 else EPSC[:, 0:1],
                                  scale=1.0 if m < 4 else 1.0 / DB).then_inc(s_rtn, 1)
                wait(t["qkr"], 2)
                store(outa["k"][lay].rearrange("a p m n -> (a p) m n"), QKB[:, 4:8, :])
                for hp in range(4):
                    for h2 in range(2):
                        h = 2 * hp + h2
                        p = mine()
                        last = ac.activation(NF[:, h % 4, 0:HALF], G[:, 2 * p, 0:HALF], ACT.Copy)
                        last = ac.activation(NF[:, h % 4, HALF:NP], G[:, 2 * p + 1, 0:NP - HALF], ACT.Copy)
                        drained(last, p)
                    for n in range(8):
                        it, i = hp * 8 + n, n % TILES
                        w = (i + 1) * P
                        wait(t["mx"])
                        ac.activation(SCR[:, it % 2, 0:w], SCR[:, it % 2, 0:w], ACT.Exp,
                                      bias=SMALL[:, 16 + it % 2:17 + it % 2],
                                      accum_out=SMALL[:, 20 + it % 2:21 + it % 2]).then_inc(s_exp, 1)
                        if n >= 1:
                            wait(t["pt"])
                            w = ((n - 1) % TILES + 1) * P
                            ac.activation(SCR[:, 2 + (it - 1) % 2, 0:w], TB[:, (it - 1) % 2, 0:w],
                                          ACT.Copy).then_inc(s_ptc, 1)
                    wait(t["pt"])
                    ac.activation(SCR[:, 2 + it % 2, 0:NP], TB[:, it % 2, :], ACT.Copy).then_inc(s_ptc, 1)
                    p = mine()
                    drained(ac.activation(YB[:, hp, 0:NP], G[:, 2 * p, :], ACT.Copy), p)
                wait(t["p"], 32)
                for g in range(2):
                    un.take()
                    wait(t["smx"])
                    ac.activation(SSC, SSC, ACT.Exp, bias=SMALL[:, 24:25], accum_out=SMALL[:, 25:26])\
                        .then_inc(s_sex, 1)
                    p = mine()
                    drained(ac.activation(PT[:, 0:8, :].rearrange("p (a b) n -> p a (b n)", a=2),
                                          G[:, 2 * p:2 * p + 2, :], ACT.Copy), p)
                    p = mine()
                    drained(ac.activation(PT[0:NS, 8, :], G[0:NS, 2 * p, 0:P], ACT.Copy), p)
                ac.wait_ge(s_outa, outs.value())
                with repeat(ac, KD, un.strides(6)):
                    for b in range(3):
                        p = mine()
                        drained(ac.activation(halves(GT[:, b, :]), both(p), ACT.Sigmoid, bias=ZERO[:, 0:1]), p)
                    un.take(3)
                un.take(KD)
                norm()
                up()
                un.take(DOWN_STEPS)
                wait(small, 11)
            ac.wait_ge(s_outa, outs.value())

        @block.vector
        def _(ve):
            un = Units()
            small = Tally(s_small, 16)
            t = {k: Tally(s) for k, s in dict(rms=s_rms, vrms=s_vrms, sp=s_sp, e=s_e, wkc=s_wkc, rowd=s_rowd, qkr=s_qkr, m=s_m,
                                              sintra=s_sintra, ses=s_ses, num=s_num, qk=s_qk, rtn=s_rtn, sc=s_sc,
                                              exp=s_exp, pt=s_pt, sex=s_sex, ss=s_ss, pv=s_pv,
                                              ).items()}
            lf = Tally(s_lf, 16)
            c0 = Tally(s_c0, 16)
            st = Tally(s_dv)

            def wait(tally, n=1):
                tally.n += n
                ve.wait_ge(tally.sem, tally.value())

            def link(ins):
                st.n += 1
                ins.then_inc(s_dv, 1)
                ve.wait_ge(s_dv, st.value())

            def mine():
                p = un.take()
                ve.wait_ge(s_unit, un.u.value())
                return p

            def both(p, m=P):
                return G[0:m, 2 * p:2 * p + 2, 0:HALF]

            def drained(ins, p):
                ins.then_inc(s_dr[p], 1)

            def by_seq(x):
                return x.rearrange("p (s t) -> p s t", t=STEPS)

            def norm(part):
                p = mine()
                wait(t["rms"])
                drained(ve.reciprocal(RS, RS), p)
                ve.wait_ge(s_dr[p], un.d[p].value())
                for k in range(KD):
                    link(ve.tensor_tensor(H[:, k, :], X[:, k, :], RS, ALU.mult))
                    ve.tensor_scalar(H[:, k, 0:NP], H[:, k, 0:NP], AMP[:, part, k, 0:1],
                                     MOD[:, part * 24 + k, 0:1], ALU.mult, ALU.add)
                    hs = by_seq(H[:, k, NP:T])
                    link(ve.tensor_tensor(hs, hs, AMP[:, part, k, 1:C][:, :, None].to_broadcast([P, SEQS, STEPS]),
                                          ALU.mult))
                    ve.tensor_tensor(hs, hs, MOD[:, part * 24 + k, 1:C][:, :, None].to_broadcast([P, SEQS, STEPS]),
                                     ALU.add).then_inc(s_h, 1)

            def up():
                with repeat(ve, KF, un.strides(2)) as m:
                    q = un.take()
                    p = mine()
                    ve.wait_ge(s_dr[q], un.d[q].value())
                    o = ACTS[:, bass.ds(m, 1), :].rearrange("p a (h n) -> p (a h) n", h=2)
                    drained(ve.tensor_tensor(o, o, both(p), ALU.mult), p)

            def add_to_x(gate):
                with repeat(ve, KD // 2, un.strides(2) | {st: 2}) as i:
                    for j in range(2):
                        p = mine()
                        xb = X[:, bass.ds(i * 2 + j, 1), :].rearrange("p a n -> p (a n)")
                        gb = MOD[:, bass.ds(i * 2 + (gate + j), 1), :].rearrange("p a n -> p (a n)")
                        ve.scalar_tensor_tensor(xb[:, 0:HALF], G[:, 2 * p, 0:HALF], gb[:, 0:1], xb[:, 0:HALF],
                                                ALU.mult, ALU.add)
                        ve.scalar_tensor_tensor(xb[:, HALF:NP], G[:, 2 * p + 1, 0:NP - HALF], gb[:, 0:1],
                                                xb[:, HALF:NP], ALU.mult, ALU.add)
                        tmp = TMP[:, j, :]
                        ve.tensor_tensor(by_seq(tmp), by_seq(G[:, 2 * p + 1, NP - HALF:HALF]),
                                         gb[:, 1:C][:, :, None].to_broadcast([P, SEQS, STEPS]), ALU.mult)\
                            .then_inc(s_dv, 1)
                        st.n += 1
                        ve.wait_ge(s_dv, st.value())
                        ve.sem_inc(s_dr[p], 1)
                        ve.tensor_tensor(xb[:, NP:T], xb[:, NP:T], tmp, ALU.add).then_inc(s_xup, 1)

            ve.memset(EPSC[:, 0:1], EPS)
            ve.memset(EPSC[:, 1:2], DB * EPS)
            ve.memset(ZERO[:], 0.0).then_inc(s_eps, 1)
            ve.memset(QS[:], 0.0)
            ve.memset(QW[:], 0.0).then_inc(s_zero, 1)
            ve.wait_ge(s_zero, 1)
            ve.sem_inc(s_wu[0], 1)
            ve.sem_inc(s_dr[0], 1)
            ve.sem_inc(s_dr[1], 1)
            ve.sem_inc(s_pgu, 4)
            ve.sem_inc(s_smallf, 1)
            ve.sem_inc(s_xup, KD)
            ve.wait_ge(s_in, 48)
            strides = un.layer() | {st: VE_LINKS, t["rms"]: 3, t["vrms"]: 5, t["sp"]: 1, t["e"]: 16, t["rowd"]: 1, t["qkr"]: 8, t["m"]: KD,
                                    t["wkc"]: 1, t["sintra"]: 1, t["ses"]: 1, t["num"]: 1, t["qk"]: 16,
                                    t["rtn"]: 8, t["sc"]: 32, t["exp"]: 32, t["pt"]: 32, t["sex"]: 2, t["ss"]: 2,
                                    t["pv"]: 2, small: 11, lf: 64, c0: 1}
            with repeat(ve, L, strides):
                wait(small, 11)
                apart(ve)
                with repeat(ve, ADA_STEPS // 2, un.strides(2)) as i:
                    for j in range(2):
                        p = mine()
                        at4 = bass.ds(i * 8 + 4 * j, 4)
                        drained(ve.tensor_tensor(MOD[:, at4, :], G[:, 2 * p, 0:4 * C].rearrange("p (b c) -> p b c", b=4),
                                                 BADA[:, at4][:, :, None].to_broadcast([P, 4, C]), ALU.add), p)
                for q in range(2):
                    ve.wait_ge(s_dr[q], un.d[q].value())
                for part in range(3):
                    o = part * 24
                    last = ve.scalar_tensor_tensor(AMP[:, part], MOD[:, o + 8:o + 16, :], 1.0,
                                                   GN[:, part, :][:, :, None].to_broadcast([P, KD, C]),
                                                   ALU.add, ALU.mult)
                    if part != 1:
                        last = ve.tensor_scalar(MOD[:, o + 16:o + 24, :], MOD[:, o + 16:o + 24, :], 0.5, None, ALU.mult)
                link(last)
                norm(0)
                up()
                add_to_x(16)
                norm(1)
                ve.tensor_tensor(WST[:], WST[:], tril01[:, None, :].to_broadcast([P, 4, P]), ALU.mult).then_inc(s_ws, 1)
                ve.tensor_tensor(WSS[:], WSS[:], seq01[:, None, :].to_broadcast([NS, 4, NS]), ALU.mult).then_inc(s_ws, 1)
                un.take(9)
                for i in range(5):
                    m = P if i < TILES else NS
                    wait(t["vrms"])
                    r = SMALL[0:m, 8 + i:9 + i]
                    link(ve.reciprocal(r, r))
                    ve.scalar_tensor_tensor(TV[0:m, i, :], TV[0:m, i, :], r, GVA[0:m, :], ALU.mult, ALU.mult)\
                        .then_inc(s_vardy, 1)
                for g in range(4):
                    p = mine()
                    a = SCR[:, 6, :].rearrange("p (n t) -> p n t", n=TILES)
                    b = TMP[:, g % 2, :]
                    ve.tensor_tensor(a, G[:, 2 * p, :].rearrange("p (n t) -> p n t", n=TILES),
                                     BS[:, g, :][:, None, :].to_broadcast([P, TILES, P]), ALU.add)
                    drained(ve.tensor_tensor(by_seq(b), by_seq(G[:, 2 * p + 1, 0:NS]),
                                             BS[:, g, 0:STEPS][:, None, :].to_broadcast([P, SEQS, STEPS]), ALU.add), p)
                    ve.wait_ge(s_dr[p], un.d[p].value())
                    ve.tensor_tensor(YA[:, g, 0:NP], YA[:, g, 0:NP], SCR[:, 6, :], ALU.mult)
                    last = ve.tensor_tensor(YA[:, g, NP:T], YA[:, g, NP:T], b, ALU.mult)
                    if g < 3:
                        link(last)
                    else:
                        last.then_inc(s_c0f, 1)
                un.take(13)
                p = mine()
                ve.tensor_scalar(halves(ROWF[0:ROWS]), both(p, ROWS), BROWS[0:ROWS, 0:1], None, ALU.add).then_inc(s_x1, 1)
                drained(ve.tensor_scalar(halves(ROWA[0:ROWS]), G[32:32 + ROWS, 2 * p:2 * p + 2, 0:HALF],
                                         BROWS[32:32 + ROWS, 0:1], None, ALU.add), p)
                ve.wait_ge(s_dr[p], un.d[p].value())
                F_, A_, M_, G_ = ROWF[0:ROWS], ROWA[0:ROWS], ROWM[0:ROWS], ROWG[0:ROWS]

                def step_of(x, k):
                    return x[:, NP + k:T:STEPS]

                wait(t["sp"])
                ve.scalar_tensor_tensor(F_, F_, 0.0, M_, ALU.min, ALU.subtract).then_inc(s_rowd, 1)
                wait(t["rowd"])
                link(ve.tensor_tensor_scan(M_[:, 0:NP], ones[0:ROWS, 0:1].to_broadcast([ROWS, NP]), F_[:, 0:NP], 0.0,
                                           ALU.mult, ALU.add))
                link(ve.tensor_copy(step_of(M_, 0), step_of(F_, 0)))
                for k in range(1, STEPS):
                    link(ve.tensor_tensor(step_of(M_, k), step_of(M_, k - 1), step_of(F_, k), ALU.add))
                link(ve.tensor_tensor(A_, A_, M_, ALU.subtract))
                link(ve.tensor_tensor_scan(G_[:, 0:NP], A_[:, 0:NP], A_[:, 0:NP], 0.0, ALU.max, ALU.max))
                link(ve.tensor_tensor(step_of(G_, 0), M0[:], step_of(A_, 0), ALU.max))
                for k in range(1, STEPS):
                    link(ve.tensor_tensor(step_of(G_, k), step_of(G_, k - 1), step_of(A_, k), ALU.max))
                ve.tensor_tensor(M_, M_, G_, ALU.add).then_inc(s_rows, 1)
                ve.tensor_tensor(by_seq(SROW[0:ROWS, 0, :]), M0[:][:, :, None].to_broadcast([ROWS, SEQS, STEPS]),
                                 by_seq(G_[:, NP:T]), ALU.subtract)
                ve.tensor_tensor(by_seq(SROW[0:ROWS, 1, :]), by_seq(A_[:, NP:T]),
                                 step_of(G_, STEPS - 1)[:, :, None].to_broadcast([ROWS, SEQS, STEPS]), ALU.subtract)\
                    .then_inc(s_wrow, 1)
                un.take(5)
                p = mine()
                ve.tensor_copy(COL[:, 0:48], G[:, 2 * p, 0:48])
                drained(ve.tensor_copy(COL[0:NS, 48:84], G[0:NS, 2 * p, 48:84]), p)
                un.take(4)
                p = mine()
                drained(ve.tensor_copy(WIB, G[:, 2 * p, 0:2 * NS].rearrange("p (h n) -> p h n", h=2)), p)
                for q in range(2):
                    ve.wait_ge(s_dr[q], un.d[q].value())
                def diag(n):
                    h, j = divmod(n, TILES)
                    ve.tensor_tensor(DIAG[:, n % 2, :], GB[:, h, j * P:(j + 1) * P], later, ALU.add).then_inc(s_diag, 1)

                diag(0)
                for h in range(HC):
                    q = un.take()
                    for j in range(TILES):
                        n = h * TILES + j
                        if n + 1 < HC * TILES:
                            diag(n + 1)
                        wait(t["e"])
                        wait(t["qk"])
                        ve.tensor_tensor(SCR[:, 2 + n % 2, j * P:NP], SCR[:, n % 2, j * P:NP], Q[:, n % 2, j * P:NP],
                                         ALU.mult).then_inc(s_wt, 1)
                    p = mine()
                    ve.wait_ge(s_dr[q], un.d[q].value())
                    d_ = SCR[:, 4, :]
                    link(ve.scalar_tensor_tensor(d_, G[:, 2 * p + 1, :], -1.0, EM[:, h % 2, :], ALU.mult, ALU.max))
                    link(ve.tensor_tensor(d_, d_, G[:, 2 * p + 1, :], ALU.max))
                    link(ve.reciprocal(d_, d_))
                    ve.tensor_tensor(SCR[:, 5, :], G[:, 2 * p, :], d_, ALU.mult).then_inc(s_dr[p], 1)
                    ve.wait_ge(s_dr[p], un.d[p].value())
                    ve.tensor_tensor(YC[:, h, 0:NP], YC[:, h, 0:NP], SCR[:, 5, :], ALU.mult).then_inc(s_yc, 1)
                wait(t["wkc"])
                for i in range(TILES):
                    kt = KCT[:, i, :].rearrange("p (h d) -> p h d", h=HC)
                    last = ve.tensor_tensor(kt, kt, WKC[:, :, i:i + 1].to_broadcast([P, HC, DKC]), ALU.mult)
                last.then_inc(s_kw, 1)
                p = mine()
                ve.tensor_copy(EM[:, 0, 0:256], G[:, 2 * p, 0:256])
                ve.tensor_copy(EM[:, 1, 0:2], G[:, 2 * p + 1, 0:2]).then_inc(s_dr[p], 1)
                ve.wait_ge(s_dr[p], un.d[p].value())
                ve.sem_inc(s_stn, 1)
                ve.tensor_tensor(ARG[0:NS], GB[0:NS, :, NP:T], seq_later[:, None, :].to_broadcast([NS, HC, NS]),
                                 ALU.add).then_inc(s_sarg, 1)
                for hp in range(2):
                    for h2 in range(2):
                        r = slice(64 * h2, 64 * h2 + 64)
                        last = ve.tensor_tensor(QW[r, hp, h2, :], QKC_[r, hp, NP:T], WIB[r, hp, :], ALU.mult)
                link(last)
                for hp in range(2):
                    for h2 in range(2):
                        last = ve.tensor_tensor(by_seq(QN[:, hp, h2, :]), by_seq(QW[:, hp, h2, :]),
                                                N0[:, hp, :][:, :, None].to_broadcast([P, SEQS, STEPS]), ALU.mult)
                ks = KCT[0:NS, TILES, :].rearrange("p (h d) -> p h d", h=HC)
                ve.tensor_tensor(ks, ks, COL[0:NS, 60 + HB:72][:, :, None].to_broadcast([NS, HC, DKC]), ALU.mult)\
                    .then_inc(s_kws, 1)
                wait(t["sintra"])
                wait(t["ses"])
                for h2 in range(2):
                    last = ve.tensor_tensor(WSM[0:NS, h2:HC:2, :], ES[0:NS, h2:HC:2, :],
                                            Q[0:NS, h2, 0:2 * NS].rearrange("p (h n) -> p h n", h=2), ALU.mult)
                last.then_inc(s_sw, 1)
                wait(t["num"])
                den = TB[:, 1, 0:HC * NS].rearrange("p (h n) -> p h n", h=HC)
                link(ve.scalar_tensor_tensor(ARG, den, -1.0, EMS, ALU.mult, ALU.max))
                link(ve.tensor_tensor(ARG, ARG, den, ALU.max))
                link(ve.reciprocal(ARG, ARG))
                link(ve.tensor_tensor(ES, TB[:, 0, 0:HC * NS].rearrange("p (h n) -> p h n", h=HC), ARG, ALU.mult))
                ve.tensor_tensor(YC[:, :, NP:T], YC[:, :, NP:T], ES, ALU.mult).then_inc(s_yc, 1)
                wait(c0)
                for hp in range(2):
                    for h2 in range(2):
                        h = 2 * hp + h2
                        ve.tensor_tensor(VBLK[0:NS, h2, :, :],
                                         TV2[0:NS, TILES, h * P:(h + 1) * P][:, None, :].to_broadcast([NS, SEQS, P]),
                                         own_seq[:, :, None].to_broadcast([NS, SEQS, P]), ALU.mult).then_inc(s_vblk, 1)
                    dec = WIB[:, hp, STEPS - 1:NS:STEPS]
                    link(ve.tensor_tensor(CS[:, hp], CS[:, hp], dec[:, :, None].to_broadcast([P, SEQS, P]), ALU.mult))
                    p = mine()
                    ve.tensor_tensor(CS[:, hp].rearrange("p (a s) v -> p a (s v)", a=2),
                                     CS[:, hp].rearrange("p (a s) v -> p a (s v)", a=2),
                                     G[:, 2 * p:2 * p + 2, :], ALU.add).then_inc(s_dr[p], 1)
                    ve.wait_ge(s_dr[p], un.d[p].value())
                    ve.sem_inc(s_stn, 1)
                link(ve.tensor_tensor(N0[:], N0[:], WIB[:, :, STEPS - 1:NS:STEPS], ALU.mult))
                p = mine()
                ve.tensor_tensor(N0[:], N0[:], G[:, 2 * p, 0:2 * SEQS].rearrange("p (h s) -> p h s", h=2), ALU.add)\
                    .then_inc(s_dr[p], 1)
                ve.wait_ge(s_dr[p], un.d[p].value())
                ve.sem_inc(s_stn, 1)
                ve.sem_inc(s_lff, 1)
                un.take(13)
                for m in range(8):
                    p = mine()
                    wait(t["rtn"])
                    drained(ve.reciprocal(RT[:, m % 2, :], RT[:, m % 2, :]), p)
                    ve.wait_ge(s_dr[p], un.d[p].value())
                    ve.scalar_tensor_tensor(QKB[:, m, :], QKB[:, m, :], GQK[:, m // 4:m // 4 + 1], RT[:, m % 2, :],
                                            ALU.mult, ALU.mult).then_inc(s_qkr, 1)
                wait(t["qkr"], 8)
                for h in range(HB):
                    r = slice(64 * (h % 2), 64 * (h % 2) + 64)
                    last = ve.tensor_copy(QS[r, h // 2, :, h, :], by_seq(QKB[r, h // 2, NP:T]))
                last.then_inc(s_qs, 1)
                for hp in range(4):
                    un.take(2)
                    for q in range(2):
                        ve.wait_ge(s_dr[q], un.d[q].value())
                    for n in range(8 + 1):
                        if n < 8:
                            it, i, h = hp * 8 + n, n % TILES, 2 * hp + n // TILES
                            w = (i + 1) * P
                            if it >= 2:
                                wait(t["pt"])
                            wait(t["sc"])
                            apart(ve)
                            link(ve.tensor_tensor_reduce(SCR[:, it % 2, 0:w], Q[:, it % 2, 0:w], NF[:, h % 4, 0:w], 1.0,
                                                         -BIG, ALU.add, ALU.max, SMALL[:, 18 + it % 2:19 + it % 2]))
                            ve.tensor_scalar(SMALL[:, 16 + it % 2:17 + it % 2], SMALL[:, 18 + it % 2:19 + it % 2], -1.0,
                                             None, ALU.mult).then_inc(s_max, 1)
                        if n >= 1:
                            it = hp * 8 + n - 1
                            w = ((n - 1) % TILES + 1) * P
                            wait(t["exp"])
                            s1 = SMALL[:, 20 + it % 2:21 + it % 2]
                            link(ve.reciprocal(s1, s1))
                            ve.tensor_scalar(SCR[:, it % 2, 0:w], SCR[:, it % 2, 0:w], s1, None, ALU.mult).then_inc(s_p, 1)
                    un.take()
                wait(t["pt"], 2)
                for g in range(2):
                    wait(lf, 32)
                    link(ve.tensor_tensor_scan(FB[:, 0:PAST], ones[:, 0:1].to_broadcast([P, PAST]), LFR, 0.0,
                                               ALU.mult, ALU.add))
                    if g == 0:
                        ve.sem_inc(s_lff, 1)
                    ve.tensor_tensor(DIAG[0:NS, g, :].rearrange("p (s h q) -> p s h q", s=4, h=HB),
                                     new_seq[:, 4 * g:4 * g + 4][:, :, None, None].to_broadcast([NS, 4, HB, STEPS]),
                                     COL[0:NS, 72:72 + HB][:, None, :, None].to_broadcast([NS, 4, HB, STEPS]),
                                     ALU.mult).then_inc(s_ln, 1)
                    p = mine()
                    drained(ve.scalar_tensor_tensor(FB[:, PAST:PAST + NS], G[:, 2 * p, 0:NS], FB[:, PAST - 1:PAST],
                                                    new_mask[:, g, :], ALU.add, ALU.subtract), p)
                    ve.wait_ge(s_dr[p], un.d[p].value())
                    wait(t["ss"])
                    ve.scalar_tensor_tensor(SSC[:, 0:PAST].rearrange("p (a n) -> p a n", a=2),
                                            FB[:, 0:PAST].rearrange("p (a n) -> p a n", a=2), -1.0, Q[:, :, :],
                                            ALU.mult, ALU.add)
                    link(ve.scalar_tensor_tensor(SSC[:, PAST:PAST + NS], FB[:, PAST:PAST + NS], -1.0, TB[:, 0, 0:NS],
                                                 ALU.mult, ALU.add))
                    link(ve.tensor_reduce(SMALL[:, 26:27], SSC, AX.X, ALU.max))
                    ve.tensor_scalar(SMALL[:, 24:25], SMALL[:, 26:27], -1.0, None, ALU.mult).then_inc(s_smx, 1)
                    wait(t["sex"])
                    link(ve.reciprocal(SMALL[:, 27:28], SMALL[:, 25:26]))
                    ve.tensor_scalar(SSC, SSC, SMALL[:, 27:28], None, ALU.mult).then_inc(s_ps, 1)
                    un.take(2)
                    wait(t["pv"])
                    for h2 in range(2):
                        r = slice(64 * h2, 64 * h2 + 64)
                        src = TB[r, 1, 0:P].rearrange("p (s k c) -> p s k c", s=4, k=4)[:, :, :, 4 * h2:4 * h2 + 4]
                        dst = YB[r, :, NP + 16 * g:NP + 16 * g + 16].rearrange("p k (s q) -> p s k q", s=4)
                        last = ve.tensor_copy(dst, src)
                    last.then_inc(s_pvc, 1)
                with repeat(ve, KD, un.strides(6) | {st: 1, t["m"]: 1}) as m:
                    un.take(3)
                    acc = ZT[:, 0, :]
                    for b in range(3):
                        p = mine()
                        if b == 0:
                            ve.wait_ge(s_dr[(p + 1) % 2], un.d[(p + 1) % 2].value())
                        z = ZT[:, 0 if b == 0 else 1, :]
                        ve.tensor_tensor(halves(z), both(p), halves(GT[:, b, :]), ALU.mult).then_inc(s_dr[p], 1)
                        ve.wait_ge(s_dr[p], un.d[p].value())
                        if b == 1:
                            link(ve.tensor_tensor(acc, acc, z, ALU.add))
                        if b == 2:
                            o = MT[:, bass.ds(m, 1), :].rearrange("p a n -> p (a n)")
                            ve.tensor_tensor(o, acc, z, ALU.add).then_inc(s_m, 1)
                            wait(t["m"])
                ve.sem_inc(s_smallf, 1)
                add_to_x(24 + 16)
                norm(2)
                up()
                add_to_x(48 + 16)


_OUTS = dict(y=(P, KD, T), k=(L, P, 4, T), v=(L, T, 512), logf=(L, HB, T), m=(L, HC, NS + 1),
             C_prompt=(L, P, 2, P), n_prompt=(L, P, 2), C_sample=(L, 2, P, SEQS, P), n_sample=(L, P, 2, SEQS),
             chunk_v=(L, NS, 512))


def lay_out(x):
    a = {k: np.asarray(v) for k, v in x.items()}

    def blocks(w, k):
        return w.reshape(L, k, P, -1).transpose(0, 2, 1, 3)

    def steps(w, k, n):
        b = blocks(w, k)
        s = b.shape[3] // n
        return b.reshape(L, P, k, s, n).transpose(0, 3, 1, 2, 4).reshape(L * s, P, k * n)

    tokens = np.concatenate([a["x_prompt"][0], a["x_sample"].reshape(NS, D)])
    cond = np.concatenate([a["c_prompt"], a["c_sample"]])
    w_in = a["w_in"]
    cut = np.cumsum([0, 512, 512, 512, 512, 512, HB, 256, 256, 512, HC, HC, 512, 3 * D])
    ua, va, qb, kb, vb, fb, qc, kc, vc, ic, fc, oc, gt = (w_in[:, :, cut[i]:cut[i + 1]] for i in range(13))
    up = a["w_ff_up"].reshape(L, 2, KD, P, 2, UP_STEPS, 256).transpose(0, 1, 5, 3, 2, 4, 6)
    down = a["w_ff_down"].reshape(L, 2, KF, P, DOWN_STEPS, P).transpose(0, 1, 4, 3, 2, 5)
    gates = gt.reshape(L, KD, P, 3, KD, P).transpose(0, 4, 2, 1, 3, 5)
    branch = a["w_branch"].reshape(L, 3, 4, P, KD, P).transpose(0, 4, 3, 1, 2, 5)
    zero = np.zeros((L, D, 20), w_in.dtype)
    b_rows = np.zeros((L, 44, 1), w_in.dtype)
    b_rows[:, 0:HB, 0], b_rows[:, HB:ROWS, 0], b_rows[:, 32 + HB:44, 0] = a["b_fb"], a["b_fc"], a["b_ic"]
    m0 = np.zeros((L, ROWS, SEQS), a["state_m"].dtype)
    m0[:, HB:] = a["state_m"].transpose(0, 2, 1)
    w_s = a["w_s"].transpose(0, 3, 1, 2)
    pool = a["cache_k"].shape[1]
    laid = dict(
        consts=constants(),
        x=tokens.T.reshape(KD, P, T).transpose(1, 0, 2),
        c=cond.T.reshape(KD, P, C).transpose(1, 0, 2),
        w_ada=steps(a["w_ada"], KD, 512),
        w_up=up.reshape(L * 2 * UP_STEPS, P, SLOT),
        w_down=down.reshape(L * 2 * DOWN_STEPS, P, KF * P),
        w_in=np.stack([steps(w, KD, 512) for w in (ua, va, np.concatenate([qc, kc], 2), vc, oc, qb, kb, vb)], 1)
        .reshape(L * 8, P, SLOT),
        w_rows=blocks(np.concatenate([fb, fc, zero, zero[:, :, :HB], ic], 2), KD),
        w_gate=gates.reshape(L * KD, P, KD * 3 * P),
        w_branch=branch.reshape(L * KD, P, 12 * P),
        w_out=steps(a["w_out"], KD, 512),
        b_ada=a["b_ada"].reshape(L, 9 * KD, P).transpose(0, 2, 1),
        g_norm=a["g_norm"].reshape(L, 3, KD, P).transpose(0, 3, 1, 2),
        g_va=a["g_va"], b_s=a["b_s"], w_s=w_s,
        w_s_new=np.tile(w_s[:, 0:STEPS, :, 0:STEPS], (1, SEQS, 1, SEQS)),
        b_rows=b_rows,
        g_qk=np.tile(np.stack([a["g_qb"], a["g_kb"]], 2), (1, 2, 1)),
        m0=m0,
        n0=a["state_n"].reshape(L, SEQS, 2, P).transpose(0, 3, 2, 1),
        C0=a["state_C"].reshape(L, SEQS, 2, 2, P, DKC).transpose(0, 3, 5, 2, 1, 4).reshape(L, P, 2, SEQS, P),
        page_table=a["page_table"].reshape(1, SEQS * PAGES),
        cache_k=a["cache_k"].reshape(L * pool, PAGE, 4, P).transpose(0, 3, 2, 1).reshape(L * pool, P, 512),
        cache_v=a["cache_v"].reshape(L * pool, PAGE, 512),
        cache_f=a["cache_logf"].reshape(L * pool, PAGE, HB).transpose(0, 2, 1),
    )
    return {k: np.ascontiguousarray(v) for k, v in laid.items()}


def results(o):
    y = o["y"].transpose(1, 0, 2).reshape(D, T).T
    k = o["k"].transpose(0, 3, 2, 1).reshape(L, T, HB, DB)
    v = o["v"].reshape(L, T, HB, DB)
    lf = o["logf"].transpose(0, 2, 1)
    cp = o["C_prompt"].reshape(L, 2, DKC, 2, P).transpose(0, 3, 1, 4, 2).reshape(L, 1, HC, DVC, DKC)
    np_ = o["n_prompt"].reshape(L, 2, DKC, 2).transpose(0, 3, 1, 2).reshape(L, 1, HC, DKC)
    cs = o["C_sample"].reshape(L, 2, 2, DKC, SEQS, P).transpose(0, 4, 1, 2, 5, 3).reshape(L, SEQS, HC, DVC, DKC)
    ns = o["n_sample"].reshape(L, 2, DKC, 2, SEQS).transpose(0, 4, 3, 1, 2).reshape(L, SEQS, HC, DKC)
    out = (y[:NP].reshape(1, NP, D), y[NP:].reshape(SEQS, STEPS, D),
           k[:, :NP].reshape(L, 1, NP, HB, DB), v[:, :NP].reshape(L, 1, NP, HB, DB), lf[:, :NP].reshape(L, 1, NP, HB),
           cp, np_, o["m"][:, :, 0].reshape(L, 1, HC),
           k[:, NP:].reshape(L, SEQS, STEPS, HB, DB), v[:, NP:].reshape(L, SEQS, STEPS, HB, DB),
           lf[:, NP:].reshape(L, SEQS, STEPS, HB), cs, ns, o["m"][:, :, STEPS::STEPS].transpose(0, 2, 1),
           o["chunk_v"].reshape(L, SEQS, STEPS, 512))
    return tuple(np.ascontiguousarray(r) for r in out)


def kernel(**inputs):
    import concourse.bacc as bacc
    from concourse.bass_utils import run_bass_kernel_spmd

    arrays = lay_out(inputs)
    nc = bacc.Bacc("TRN2", target_bir_lowering=False, num_devices=1)
    d = {k: nc.dram_tensor("in_" + k, v.shape, mybir.dt.from_np(v.dtype), kind="ExternalInput").ap() for k, v in arrays.items()}
    d["outs"] = {k: nc.dram_tensor("out_" + k, s, F32, kind="ExternalOutput").ap() for k, s in _OUTS.items()}
    build(nc, d, d["outs"])
    r = run_bass_kernel_spmd(nc, [{"in_" + k: v for k, v in arrays.items()}], core_ids=[0]).results[0]
    return results({k: np.asarray(r["out_" + k]) for k in _OUTS})
```

```python
from contextlib import ExitStack, contextmanager

import numpy as np

import concourse.bass as bass
from concourse import mybir

F32 = mybir.dt.float32
F32R = mybir.dt.float32r
I32 = mybir.dt.int32
ACT = mybir.ActivationFunctionType
ALU = mybir.AluOpType
AX = mybir.AxisListType

P = 128
L = 2
D = 1024
KD = D // P
NP = 512
SEQS, STEPS = 8, 4
NS = SEQS * STEPS
T = NP + NS
HALF = T // 2
TILES = NP // P
C = 1 + SEQS
FF = 2816
KF = FF // P
PAGES, PAGE = 8, 128
PAST = PAGES * PAGE
POOL = 80
HB, DB = 8, 64
HC, DKC, DVC = 4, 64, 128
ROWS = HB + HC
BIG = 1.0e30
EPS = 1e-6
SLOT = 4096
AREA = 29128
ADA_STEPS, OUT_STEPS = 18, 2
FF_PART = (12, 10)
UP_STEPS = tuple(n // 2 for n in FF_PART)
DOWN_STEPS = KD // 2
UP_BLOCK = KD * P
RING = max(FF_PART) * P

_CONSTS = dict(ident=P, ones=P, halfones=P, later=P, earlier=P, tril01=P, sel_neg=ROWS * P, sel_pair=2 * P,
               seq_later=NS, fold=C, seq01=NS, own_seq=SEQS, new_mask=2 * NS, new_seq=2 * 4)
CONST_AT, _n = {}, 0
for _k, _w in _CONSTS.items():
    CONST_AT[_k] = (_n, _w)
    _n += _w
CONST_W = _n


def constants():
    c = np.zeros((P, CONST_W), np.float32)

    def put(name, a):
        at, w = CONST_AT[name]
        a = a.reshape(a.shape[0], -1)
        assert a.shape[1] == w
        c[:a.shape[0], at:at + w] = a

    i = np.arange(P)
    put("ident", np.eye(P))
    put("ones", np.ones((P, P)))
    put("halfones", (i[:, None] // 64 == i[None] // 64) * 1.0)
    put("later", np.where(i[None] >= i[:, None], 0, -BIG))
    put("earlier", np.where(i[None] <= i[:, None], 0, -BIG))
    put("tril01", (i[None] >= i[:, None]) * 1.0)
    sel = np.zeros((ROWS, ROWS, P))
    for r in range(ROWS):
        sel[r, r] = -1 if r >= HB else 1
    put("sel_neg", sel)
    pair = np.zeros((ROWS, 2, P))
    for h in range(HC):
        pair[HB + h, h // 2, 64 * (h % 2):64 * (h % 2) + 64] = 1
    put("sel_pair", pair)
    t = np.arange(NS)
    same = t[:, None] // STEPS == t[None] // STEPS
    put("fold", np.arange(2 * C)[:, None] % C == np.arange(C)[None])
    put("seq_later", np.where(same & (t[None] >= t[:, None]), 0, -BIG))
    put("seq01", (same & (t[None] >= t[:, None])) * 1.0)
    put("own_seq", (t[:, None] // STEPS == np.arange(SEQS)[None]) * 1.0)
    new = np.full((P, 2, NS), -BIG)
    for g in range(2):
        own = (t[None] // STEPS == 4 * g + i[:, None] // 32) & (t[None] % STEPS <= i[:, None] % STEPS)
        new[:, g][own] = 0
    put("new_mask", new)
    put("new_seq", (t[:, None] // STEPS == np.arange(8)[None]) * 1.0)
    return c


class Tally:

    def __init__(self, sem, unit=1, seed=0):
        self.sem, self.unit, self.n, self.loops = sem, unit, seed, []

    def value(self, ahead=0):
        v = (self.n + ahead) * self.unit
        for reg, stride in self.loops:
            v = reg * (stride * self.unit) + v
        return v


@contextmanager
def repeat(eng, count, strides):
    before = {t: t.n for t in strides}
    with eng.Fori(0, count) as i:
        for t, s in strides.items():
            t.loops.append((i, s))
        yield i
        for t, s in strides.items():
            assert t.n - before[t] == s, (str(t.sem), t.n - before[t], s)
            t.loops.pop()
            t.n += s * (count - 1)


UA, VA, QKC, VC, OC, QB, KB, VB = range(8)

VE_LINKS = 268

UNITS = dict(ada=2 * ADA_STEPS, norm=1, up=2 * KF, down=2 * KD,
             gate=4 + 5 + 4, mlstm_in=4 + 5 + 4 + 1 + 5 + 1 + 4 + 1, mlstm=2 * HC + 1 + 2 + 1,
             fox_in=4 + 4 + 5 + 8, fox=HB + HB // 2, fox_sample=2 * 3, merge=6 * KD, out=KD)
FFN_UNITS = ([1 + 4] + [4] * (UP_STEPS[0] - 1) + [2] * DOWN_STEPS + [4] * UP_STEPS[1] + [2] * DOWN_STEPS)
STEP_UNITS = ([1, 1] + [2] * (ADA_STEPS - 2) + [2 + FFN_UNITS[0]] + FFN_UNITS[1:]
              + [1 + 4, 5, 4 + 4, 5, 4, 1 + 5 + 1 + 4 + 1 + 2 * HC + 1 + 2 + 1 + 4, 4, 5]
              + [8 + HB + HB // 2 + 2 * 3 + 3, 3] + [3, 3] * (KD - 1) + [4] * OUT_STEPS
              + FFN_UNITS)
UNITS_L = sum(UNITS[k] for k in UNITS) + 2 + UNITS["up"] + UNITS["down"]
FFN_STEPS = sum(UP_STEPS) + 2 * DOWN_STEPS
STEPS_L = ADA_STEPS + 2 * FFN_STEPS + 8 + 2 * KD + OUT_STEPS

FFN_SPLITS = [4] * UP_STEPS[0] + [2] * DOWN_STEPS + [4] * UP_STEPS[1] + [2] * DOWN_STEPS
STEP_SPLITS = [1] * ADA_STEPS + FFN_SPLITS + [0] * (STEPS_L - ADA_STEPS - 2 * FFN_STEPS) + FFN_SPLITS


def ffn_plan():
    plan, step = [], 0
    for part, blocks in enumerate(FF_PART):
        plan += [(step + i // 4, i % 4 * UP_BLOCK, UP_BLOCK) for i in range(2 * blocks)]
        step += UP_STEPS[part]
        plan += [(step + i // 2, i % 2 * blocks * P, blocks * P) for i in range(KD)]
        step += DOWN_STEPS
    return plan


def build(nc, d, out):
    ctx = ExitStack()
    with ctx:
        top = [-(-nc.sbuf_base // 64) * 64]

        def sb(name, shape, dt=F32, over=None):
            o = top[0] if over is None else over
            if over is None:
                top[0] += -(-4 * int(np.prod(shape[1:])) // 32) * 32
            return nc.alloc_sbuf_tensor_at(name, shape, dt, offset=o)

        def sem(name):
            return ctx.enter_context(nc.semaphore(name))

        cst = sb("cst", [P, CONST_W])
        W = [sb(f"w{i}", [P, SLOT]) for i in range(2)]
        X = sb("x", [P, KD, T])
        h_at = top[0]
        H = sb("h", [P, KD, T])
        HH = sb("h_hi", [P, KD, T], F32R, over=h_at)
        MOD = sb("mod", [P, 9 * KD, C])
        AMP = sb("amp", [P, 3, KD, C])
        COND = sb("cond", [P, KD, C])
        CHL = sb("cond_hi_lo", [P, KD, 2 * C], F32R)
        BADA = sb("bada", [P, 9 * KD])
        GN = sb("gn", [P, 3, KD])
        GVA = sb("gva", [P, 512])
        BS = sb("bs", [P, 4, P])
        WST = sb("wst", [P, 4, P])
        WSS = sb("wss", [NS, 4, NS])
        BROWS = sb("brows", [44, 1])
        GQK = sb("gqk", [P, 2])
        WFI = sb("wfi", [P, KD, 44])
        M0 = sb("m0", [ROWS, SEQS])
        N0 = sb("n0", [P, 2, SEQS])
        TABLE = sb("table", [1, SEQS * PAGES], I32)
        EPSC = sb("epsc", [P, 2])
        ZERO = sb("zero", [P, 1])
        QS = sb("qs", [P, 4, SEQS, HB, STEPS])
        QW = sb("qw", [P, 2, 2, NS])
        area_at = top[0]
        area = sb("area", [P, AREA])

        def over(name, start, *shape, dt=F32R):
            return sb(name, [P] + list(shape), dt, over=area_at + 4 * start)

        WHA = [over(f"ada_w_hi{i}", i * SLOT, SLOT) for i in range(2)]
        WLA = [over(f"ada_w_lo{i}", (2 + i) * SLOT, SLOT) for i in range(2)]
        o_f = 2 * FF_PART[0] * T
        AH = over("acts_hi", 0, FF_PART[0], T)
        AL = over("acts_lo", FF_PART[0] * T, FF_PART[0], T)
        HL = over("h_lo", o_f, KD, T)
        o_f += KD * T
        WH = [over(f"w_hi{i}", o_f + i * RING, RING) for i in range(2)]
        WL = [over(f"w_lo{i}", o_f + (2 + i) * RING, RING) for i in range(2)]
        o_f += 4 * RING
        at = [0]

        def take(*shape, start=None):
            n = int(np.prod(shape))
            o = at[0] if start is None else start
            if start is None:
                at[0] += n
                assert at[0] <= AREA, at[0]
            v = area[:, o:o + n]
            names = "abcd"[:len(shape)]
            if len(shape) > 1:
                v = v.rearrange(f"p ({' '.join(names)}) -> p {' '.join(names)}",
                                **{k: s for k, s in zip(names[1:], shape[1:])})
            return v, o

        YS, _ = take(3, 4, T)
        YA, YB, YC = YS[:, 0], YS[:, 1], YS[:, 2]
        QKB, o_qk = take(8, T)
        QKC_, _ = take(4, T, start=o_qk + 4 * T)
        ROWG, _ = take(T, start=o_qk)
        ROWM, _ = take(T, start=o_qk + T)
        SROW, _ = take(3, NS, start=o_qk + 2 * T)
        MT, _ = take(KD, T, start=o_qk)
        TV, o_tv = take(5, 512)
        CS, _ = take(2, SEQS, P, start=o_tv)
        TV2, _ = take(5, 512)
        ROWA, _ = take(T)
        ROWF, _ = take(T)
        COL, _ = take(84)
        KCT, o_k = take(5, 256)
        EM, _ = take(2, 512)
        NF, _ = take(4, 512, start=o_k)
        GB, o_g = take(4, T)
        FB, _ = take(PAST + NS, start=o_g)
        LFR, _ = take(PAST, start=o_g + PAST + NS)
        SCR, o_s = take(8, 512)
        SSC, _ = take(PAST + NS, start=o_s)
        PT, _ = take(9, P, start=o_s + PAST + NS)
        RT, _ = take(2, T, start=o_s)
        SQ, _ = take(2, T, start=o_s + 2 * T)
        GT, _ = take(3, T, start=o_s)
        ZT, _ = take(2, T, start=o_s + 3 * T)
        VBLK, _ = take(2, SEQS, P, start=o_s)
        PG, _ = take(4, 512)
        PLACES = [PG[:, i] for i in range(4)] + [NF[:, i] for i in range(4)]
        EMS, _ = take(4, NS)
        WIB, _ = take(2, NS)
        QN, _ = take(2, 2, NS)
        ARG, _ = take(4, NS)
        ES, _ = take(4, NS)
        WSM, _ = take(4, NS)
        WKC, _ = take(4, TILES)
        DIAG, _ = take(2, P)
        SMALL, _ = take(32)
        TMP, _ = take(2, NS)
        MR, _ = take(2, 4 * P, start=4 * SLOT)
        SIL, _ = take(2, T, start=o_f)
        PR, _ = take(T, start=o_f + 2 * T)
        TN, _ = take(2, T, start=o_f + 3 * T)
        RS, _ = take(T, start=o_f + 5 * T)

        G = ctx.enter_context(nc.psum_tensor("g", [P, 4, 512], F32))
        Q = ctx.enter_context(nc.psum_tensor("q", [P, 2, 512], F32))
        TB = ctx.enter_context(nc.psum_tensor("tb", [P, 2, 512], F32))

        def const(name, rows=P):
            a, w = CONST_AT[name]
            return cst[0:rows, a:a + w]

        ident, ones, halfones = const("ident"), const("ones"), const("halfones")
        fold = const("fold", 2 * C)
        later, earlier, tril01 = const("later"), const("earlier"), const("tril01")
        sel_neg = const("sel_neg", ROWS).rearrange("p (r n) -> p r n", n=P)
        sel_pair = const("sel_pair", ROWS).rearrange("p (r n) -> p r n", n=P)
        seq_later, seq01, own_seq = const("seq_later", NS), const("seq01", NS), const("own_seq", NS)
        new_mask = const("new_mask").rearrange("p (g n) -> p g n", g=2)
        new_seq = const("new_seq", NS)

        s_in = sem("inputs_in")
        s_eps = sem("eps_set")
        s_zero = sem("spread_zeroed")
        s_cond = sem("cond_silu")
        s_unit = sem("unit_done")
        s_dr = [sem("drained0"), sem("drained1")]
        s_w = [sem("weights_in0"), sem("weights_in1")]
        s_small = sem("small_in")
        s_smallf = sem("small_used")
        s_sq = sem("squares")
        s_rms = sem("root_ms")
        s_h = sem("h_ready")
        s_mr = sem("vector_rows")
        s_tn = sem("h_value")
        s_hh = sem("h_hi_ready")
        s_wh = sem("weights_hi")
        s_wl = sem("weights_split")
        s_acts = sem("acts_split")
        s_mods = sem("mods_ready")
        s_vrms = sem("va_rms")
        s_vardy = sem("va_ready")
        s_chunkv = sem("chunk_v_out")
        s_ws = sem("w_s_masked")
        s_x1 = sem("gate_rows")
        s_sp = sem("softplus_rows")
        s_rowd = sem("row_diff")
        s_rows = sem("rows_ready")
        s_wrow = sem("weight_rows")
        s_exr = sem("exp_rows")
        s_qk = sem("mlstm_scores")
        s_diag = sem("diag_ready")
        s_e = sem("decay_ready")
        s_wt = sem("mlstm_weights")
        s_yc = sem("yc_head")
        s_wkc = sem("key_weights")
        s_kw = sem("weighted_keys")
        s_sintra = sem("sample_scores")
        s_sarg = sem("sample_args")
        s_ses = sem("sample_decay")
        s_sw = sem("sample_weights")
        s_c0 = sem("state_in")
        s_c0f = sem("state_free")
        s_num = sem("sample_num")
        s_vblk = sem("v_spread")
        s_kws = sem("sample_weighted_keys")
        s_st = sem("state_out")
        s_stn = sem("state_new")
        s_sqn = sem("qk_squares")
        s_rtn = sem("qk_root")
        s_qkr = sem("qk_ready")
        s_sc = sem("fox_scores")
        s_nf = sem("fox_bias")
        s_max = sem("fox_max")
        s_exp = sem("fox_exp")
        s_p = sem("fox_probs")
        s_pt = sem("fox_turned")
        s_ptc = sem("fox_turned_copied")
        s_hpd = sem("fox_pair_done")
        s_lf = sem("past_logf_in")
        s_lff = sem("past_logf_used")
        s_pg = [sem(f"page_in{i}") for i in range(8)]
        s_pgo = [sem(f"page_in{i}_by_sp") for i in range(1, 8, 2)]
        s_pgu = sem("pages_used")
        s_qs = sem("queries_spread")
        s_ln = sem("new_logf_spread")
        s_ss = sem("sample_fox_scores")
        s_smx = sem("sample_fox_max")
        s_sex = sem("sample_fox_exp")
        s_ps = sem("sample_fox_probs")
        s_pv = sem("sample_fox_out")
        s_pvc = sem("sample_fox_kept")
        s_xup = sem("x_updated")
        s_gt = sem("merge_gates")
        s_m = sem("merged")
        s_out = sem("outputs_out")
        s_outa = sem("outputs_out_act")
        s_dv = sem("vector_step")
        s_ac = sem("scalar_step")
        s_ada = sem("ada_bias_added")

        s_apart = sem("wait_apart")

        block = ctx.enter_context(nc.Block())

        def apart(eng):
            eng.sem_inc(s_apart, 1)

        class Units:

            def __init__(self):
                self.u, self.d, self.k = Tally(s_unit, seed=2), [Tally(s_dr[0], seed=1), Tally(s_dr[1], seed=1)], 0

            def take(self, n=1):
                for _ in range(n):
                    p = self.k % 2
                    self.k += 1
                    self.u.n += 1
                    self.d[p].n += 1
                return p

            def layer(self):
                assert UNITS_L % 2 == 0 and UNITS_L == sum(STEP_UNITS)
                return self.strides(UNITS_L)

            def strides(self, n):
                assert n % 2 == 0
                return {self.u: n, self.d[0]: n // 2, self.d[1]: n // 2}

        def halves(x):
            return x.rearrange("p (a n) -> p a n", a=2)

        def load_pages(eng, pages, cache, l, g, mine):
            with repeat(eng, 4, {pages: 8}) as i:
                for place in range(8):
                    pages.n += 1
                    if place in mine:
                        r = eng.value_load(TABLE[0:1, bass.ds(i * 8 + (g * 32 + place), 1)], min_val=0,
                                           max_val=POOL - 1)
                        eng.wait_ge(s_pgu, pages.value())
                        eng.dma_start(PLACES[place], d[cache][bass.ds(l * POOL + r, 1)]
                                      .rearrange("a p n -> (a p) n"))\
                            .then_inc(s_pgo[place // 2] if place % 2 and len(mine) == 8 else s_pg[place], 16)

        EVEN, ODD = range(0, 8, 2), range(1, 8, 2)

        @block.sync
        def _(sp):
            sp.dma_start(TABLE[:], d["page_table"]).then_inc(s_in, 16)
            sp.wait_ge(s_in, 16)
            sp.dma_start(cst[:], d["consts"]).then_inc(s_in, 16)
            sp.dma_start(COND[:], d["c"]).then_inc(s_in, 16)
            sp.dma_start(X[:], d["x"]).then_inc(s_in, 16)
            done = Tally(s_unit, seed=2)
            split = Tally(s_wl)
            pages = Tally(s_pgu)
            k = [0]

            def load(src, n):
                at = k[0] % STEPS_L
                done.n += STEP_UNITS[(at - 2) % STEPS_L]
                split.n += STEP_SPLITS[(at - 2) % STEPS_L]
                if at >= 2 and STEP_SPLITS[at - 2]:
                    sp.wait_ge(s_wl, split.value())
                else:
                    sp.wait_ge(s_unit, done.value())
                sp.dma_start(W[at % 2][:, 0:n], src.rearrange("a p n -> (a p) n")).then_inc(s_w[at % 2], 16)
                k[0] += 1

            def stream(name, n_steps, size, base):
                head = 4 - n_steps % 2
                for j in range(min(head, n_steps)):
                    load(d[name][bass.ds(base + j, 1)], size)
                if n_steps > head:
                    rounds = (n_steps - head) // 2
                    two = [(k[0] + q - 2) % STEPS_L for q in range(2)]
                    with repeat(sp, rounds, {done: sum(STEP_UNITS[q] for q in two),
                                             split: sum(STEP_SPLITS[q] for q in two)}) as i:
                        for j in range(2):
                            load(d[name][bass.ds(base + i * 2 + (head + j), 1)], size)
                    k[0] += 2 * (rounds - 1)

            done.n -= sum(STEP_UNITS[-2:])
            split.n -= sum(STEP_SPLITS[-2:])
            with repeat(sp, L, {done: UNITS_L, split: sum(STEP_SPLITS), pages: 2 * SEQS * PAGES + 4}) as l:
                stream("w_ada", ADA_STEPS, SLOT, l * ADA_STEPS)
                ups = sum(UP_STEPS)
                for f in range(2):
                    if f == 1:
                        for n in range(8):
                            load(d["w_in"][bass.ds(l * 8 + n, 1)], SLOT)
                        for m in range(2):
                            load(d["w_gate"][bass.ds(l * KD + m, 1)], KD * 3 * P)
                            load(d["w_branch"][bass.ds(l * KD + m, 1)], 12 * P)
                            if m == 0:
                                load_pages(sp, pages, "cache_k", l, 0, EVEN)
                                load_pages(sp, pages, "cache_k", l, 1, range(8))
                                load_pages(sp, pages, "cache_v", l, 0, EVEN)
                                load_pages(sp, pages, "cache_v", l, 1, EVEN)
                                pages.n += 4
                        with repeat(sp, KD - 2, {done: 6}) as m:
                            load(d["w_gate"][bass.ds(l * KD + m + 2, 1)], KD * 3 * P)
                            load(d["w_branch"][bass.ds(l * KD + m + 2, 1)], 12 * P)
                        k[0] += 2 * (KD - 3)
                        stream("w_out", OUT_STEPS, SLOT, l * OUT_STEPS)
                    for part, blocks in enumerate(FF_PART):
                        stream("w_up", UP_STEPS[part], SLOT, (l * 2 + f) * ups + part * UP_STEPS[0])
                        stream(f"w_down{part}", DOWN_STEPS, 2 * blocks * P, (l * 2 + f) * DOWN_STEPS)
                assert k[0] == STEPS_L
            sp.wait_ge(s_xup, KD + L * 3 * KD)
            sp.dma_start(out["y"], X[:]).then_inc(s_out, 16)
            sp.wait_ge(s_out, 16)

        @block.gpsimd
        def _(po):
            po.wait_ge(s_in, 16)
            small_free = Tally(s_smallf)
            lf_free = Tally(s_lff)
            c0f = Tally(s_c0f)
            pages = Tally(s_pgu)
            with repeat(po, L, {small_free: 1, lf_free: 2, c0f: 1, pages: 2 * SEQS * PAGES + 4}) as l:
                small_free.n += 1
                po.wait_ge(s_smallf, small_free.value())
                for dst, name in ((BADA[:], "b_ada"), (GN[:], "g_norm"), (GVA[:], "g_va"), (BS[:], "b_s"),
                                  (WST[:], "w_s"), (WSS[:], "w_s_new"), (BROWS[:], "b_rows"), (GQK[:], "g_qk"),
                                  (WFI[:], "w_rows"), (M0[:], "m0"), (N0[:], "n0")):
                    src = d[name][bass.ds(l, 1)]
                    if name == "g_va":
                        src = src.rearrange("a n -> (a n)")[None, :].to_broadcast([P, 512])
                    elif name == "b_s":
                        src = src.rearrange("a g n -> (a g) n")[None, :, :].to_broadcast([P, 4, P])
                    elif len(src.shape) == 3:
                        src = src.rearrange("a p n -> (a p) n")
                    else:
                        src = src.rearrange("a p g n -> (a p) g n")
                    po.dma_start(dst, src).then_inc(s_small, 16)
                c0f.n += 1
                po.wait_ge(s_c0f, c0f.value())
                po.dma_start(CS, d["C0"][bass.ds(l, 1)].rearrange("a p h s v -> (a p) h s v")).then_inc(s_c0, 16)
                for g in range(2):
                    if g == 1:
                        load_pages(po, pages, "cache_k", l, 0, ODD)
                        pages.n += 32
                    lf_free.n += 1
                    po.wait_ge(s_lff, lf_free.value())
                    apart(po)
                    for s in range(4):
                        with po.Fori(0, PAGES) as pg:
                            r = po.value_load(TABLE[0:1, bass.ds(pg + (g * 4 + s) * PAGES, 1)], min_val=0,
                                              max_val=POOL - 1)
                            src = d["cache_f"][bass.ds(l * POOL + r, 1)].rearrange("a h n -> (a h) n")
                            po.dma_start(LFR[32 * s:32 * s + 32, bass.ds(pg * PAGE, PAGE)],
                                         src[:, None, :].to_broadcast([HB, STEPS, PAGE])).then_inc(s_lf, 16)
                load_pages(po, pages, "cache_v", l, 0, ODD)
                load_pages(po, pages, "cache_v", l, 1, ODD)
                pages.n += 4

        @block.tensor
        def _(pe):
            un = Units()
            w_in = [Tally(s_w[0], 16), Tally(s_w[1], 16)]
            hr = Tally(s_h)
            sq = Tally(s_sq)
            wl = Tally(s_wl)
            acts = Tally(s_acts)
            mr = Tally(s_mr)
            small = Tally(s_small, 16)
            t = {k: Tally(s) for k, s in dict(vardy=s_vardy, ws=s_ws, rows=s_rows, wrow=s_exr, e=s_wt, kw=s_kw,
                                               sw=s_sw, vblk=s_vblk, kws=s_kws, sqn=s_sqn, qkr=s_qkr, mx=s_max,
                                               p=s_p, ptc=s_ptc, qs=s_qs, ln=s_ln, ps=s_ps, smx=s_smx, pvc=s_pvc,
                                               m=s_m).items()}
            c0 = Tally(s_c0, 16)
            pin_sp = [Tally(s, 16) for s in s_pgo]
            pin = [Tally(s_pg[i], 16) for i in range(8)]
            step = [0]

            def wait(tally, n=1):
                tally.n += n
                pe.wait_ge(tally.sem, tally.value())

            def mm(o, a, b, start, stop, **kw):
                return pe.matmul(o, a, b, start=start, stop=stop, skip_group_check=True, **kw)

            def turn(o, a, idn):
                return pe.transpose(o, a, idn)

            def unit():
                p = un.k % 2
                pe.wait_ge(s_dr[p], un.d[p].value())
                un.take()
                return p

            def weights():
                s = step[0] % 2
                step[0] += 1
                wait(w_in[s])
                return s

            def pass_steps(n):
                for _ in range(n):
                    w_in[step[0] % 2].n += 1
                    step[0] += 1

            def product(p, blocks, rhs, m=P, first=None):
                n = len(blocks)
                for k in range(n):
                    if first is not None:
                        wait(first)
                    for h in range(2):
                        last = mm(G[0:m, 2 * p + h, 0:HALF], blocks[k], rhs(k)[:, h * HALF:(h + 1) * HALF],
                                  k == 0, k == n - 1)
                last.then_inc(s_unit, 1)

            def norm_sums():
                p = unit()
                product(p, [ones] * KD, lambda k: H[:, k, :], first=sq)

            def hk(k):
                return H[:, k, :]

            def split_product(p, r, blocks, hi, lo, first=None):
                wait(wl)
                for k in range(blocks):
                    if first is not None:
                        wait(first)
                    for i, (w, x) in enumerate(((WH, hi), (WH, lo), (WL, hi))):
                        for h in range(2):
                            last = mm(G[:, 2 * p + h, 0:HALF], w[r][:, k * P:(k + 1) * P],
                                      x[:, k, h * HALF:(h + 1) * HALF], k + i == 0, k == blocks - 1 and i == 2)
                last.then_inc(s_unit, 1)

            def ffn():
                for part, blocks in enumerate(FF_PART):
                    if part == 0:
                        split_product(unit(), 0, KD, HH, HL, first=hr)
                        split_product(unit(), 1, KD, HH, HL)
                    with repeat(pe, blocks - (part == 0), un.strides(2) | {wl: 2}):
                        for r in range(2):
                            split_product(unit(), r, KD, HH, HL)
                    split_product(unit(), 0, blocks, AH, AL, first=acts)
                    split_product(unit(), 1, blocks, AH, AL)
                    with repeat(pe, KD // 2 - 1, un.strides(2) | {wl: 2}):
                        for r in range(2):
                            split_product(unit(), r, blocks, AH, AL)
                pass_steps(FFN_STEPS)

            def project(blocks, first=None):
                s = weights()
                w = W[s][:, :].rearrange("p (k n) -> p k n", k=KD)
                for b in range(blocks):
                    product(unit(), [w[:, k, b * P:(b + 1) * P] for k in range(KD)], hk,
                            first=first if b == 0 else None)

            def project_tokens():
                s = weights()
                for i in range(5):
                    p, m = unit(), P if i < TILES else NS
                    for k in range(KD):
                        last = mm(G[0:m, 2 * p, :], H[:, k, i * P:i * P + m], W[s][:, k * 512:(k + 1) * 512],
                                  k == 0, k == KD - 1)
                    last.then_inc(s_unit, 1)

            pe.wait_ge(s_in, 64)
            strides = un.layer() | {w_in[0]: STEPS_L // 2, w_in[1]: STEPS_L // 2, hr: 3 * KD, sq: 3 * KD, small: 11,
                                    wl: ADA_STEPS + 2 * len(ffn_plan()), acts: 2 * KF, mr: ADA_STEPS,
                                    t["vardy"]: 5, t["ws"]: 2, t["rows"]: 1, t["wrow"]: 1, t["e"]: 16, t["kw"]: 1,
                                    t["sw"]: 1, t["vblk"]: 4, t["kws"]: 1, t["sqn"]: 8, t["qkr"]: 8, t["mx"]: 32,
                                    t["p"]: 32, t["ptc"]: 32, t["qs"]: 1, t["ln"]: 2, t["ps"]: 2, t["smx"]: 2,
                                    t["pvc"]: 2, t["m"]: KD, c0: 1}
            strides |= {q: 2 * SEQS if i % 2 == 0 else 2 * SEQS - 4 for i, q in enumerate(pin)} | {q: 4 for q in pin_sp}
            pe.wait_ge(s_cond, 3)
            with repeat(pe, L, strides):
                def vectors(s):
                    p = unit()
                    wait(wl)
                    for k in range(KD):
                        at4 = slice(k * 4 * P, (k + 1) * 4 * P)
                        mm(G[0:2 * C, 2 * p, :], CHL[:, k, :], WHA[s][:, at4], k == 0, False)
                        last = mm(G[0:C, 2 * p, :], CHL[:, k, 0:C], WLA[s][:, at4], False, k == KD - 1)
                    last.then_inc(s_unit, 1)

                def features(s):
                    p = unit()
                    wait(mr)
                    for b in range(4):
                        last = mm(G[:, 2 * p, b * C:(b + 1) * C], MR[0:2 * C, s, b * P:(b + 1) * P], fold, True, True)
                    last.then_inc(s_unit, 1)

                vectors(0)
                with repeat(pe, ADA_STEPS // 2 - 1, un.strides(4) | {wl: 2, mr: 2}):
                    for s in range(2):
                        vectors(1 - s)
                        features(s)
                vectors(1)
                features(0)
                features(1)
                pass_steps(ADA_STEPS)
                norm_sums()
                ffn()
                norm_sums()
                project(4, first=hr)
                project_tokens()
                wait(small, 11)
                wait(t["ws"], 2)
                wait(t["vardy"], 5)
                for g in range(4):
                    p = unit()
                    for n in range(TILES):
                        mm(G[:, 2 * p, n * P:(n + 1) * P], TV[:, n, g * P:(g + 1) * P], WST[:, g, :], True, True)
                    mm(G[:, 2 * p + 1, 0:NS], TV[0:NS, TILES, g * P:(g + 1) * P], WSS[:, g, :], True, True)\
                        .then_inc(s_unit, 1)
                project(4)
                project_tokens()
                project(4)
                p = unit()
                product(p, [WFI[:, k, :] for k in range(KD)], hk, m=44)
                for i in range(5):
                    p, m = unit(), P if i < TILES else NS
                    for hp in range(2):
                        last = turn(G[0:m, 2 * p, hp * P:(hp + 1) * P], QKC_[:, 2 + hp, i * P:i * P + m], ident)
                    last.then_inc(s_unit, 1)
                wait(t["rows"])
                wait(t["wrow"])
                p = unit()
                apart(pe)
                for i in range(5):
                    m = P if i < TILES else NS
                    turn(G[0:m, 2 * p, i * 12:i * 12 + 12], ROWA[0:ROWS, i * P:i * P + m], ident[0:ROWS, 0:ROWS])
                turn(G[0:NS, 2 * p, 60:72], SROW[0:ROWS, 1, :], ident[0:ROWS, 0:ROWS])
                turn(G[0:NS, 2 * p, 72:84], ROWF[0:ROWS, NP:T], ident[0:ROWS, 0:ROWS]).then_inc(s_unit, 1)
                for h in range(HC):
                    product(unit(), [sel_neg[:, HB + h, :]], lambda k: ROWG[0:ROWS, :])
                p = unit()
                for hp in range(2):
                    last = mm(G[:, 2 * p, hp * NS:(hp + 1) * NS], sel_pair[:, hp, :], SROW[0:ROWS, 0, :], True, True)
                last.then_inc(s_unit, 1)
                items = [(h, j) for h in range(HC) for j in range(TILES)]
                pair = [None]

                def qk(n):
                    h, j = items[n]
                    r = slice(64 * (h % 2), 64 * (h % 2) + 64)
                    mm(Q[:, n % 2, j * P:NP], QKC_[r, 2 + h // 2, j * P:(j + 1) * P], QKC_[r, h // 2, j * P:NP],
                       True, True).then_inc(s_qk, 1)

                def weigh(n):
                    h, j = items[n]
                    wait(t["e"])
                    if j == 0:
                        pair[0] = unit()
                    p, w = pair[0], SCR[:, 2 + n % 2, j * P:NP]
                    mm(G[:, 2 * p, j * P:NP], TV2[:, j, h * P:(h + 1) * P], w, j == 0, j == TILES - 1)
                    last = mm(G[:, 2 * p + 1, j * P:NP], ones, w, j == 0, j == TILES - 1)
                    if j == TILES - 1:
                        last.then_inc(s_unit, 1)

                for h in range(HC):
                    for j in range(TILES):
                        n = h * TILES + j
                        if n == 0:
                            product(unit(), [sel_neg[:, HB, :]], lambda k: ROWM[0:ROWS, :])
                            qk(0)
                        if n + 1 < len(items):
                            qk(n + 1)
                        weigh(n)
                        if j == TILES - 1 and h + 1 < HC:
                            product(unit(), [sel_neg[:, HB + h + 1, :]], lambda k: ROWM[0:ROWS, :])
                wait(t["kw"])
                p = unit()
                for h in range(HC):
                    r = slice(64 * (h % 2), 64 * (h % 2) + 64)
                    for j in range(TILES):
                        mm(G[r, 2 * p, (h // 2) * P:(h // 2 + 1) * P], KCT[:, j, h * 64:(h + 1) * 64],
                           TV2[:, j, h * P:(h + 1) * P], j == 0, j == TILES - 1)
                for hp in range(2):
                    for j in range(TILES):
                        last = mm(G[:, 2 * p + 1, hp:hp + 1], KCT[:, j, hp * P:(hp + 1) * P], ones[:, 0:1],
                                  j == 0, j == TILES - 1)
                last.then_inc(s_unit, 1)
                for h in range(HC):
                    r = slice(64 * (h % 2), 64 * (h % 2) + 64)
                    last = mm(Q[0:NS, h % 2, (h // 2) * NS:(h // 2 + 1) * NS], QKC_[r, 2 + h // 2, NP:T],
                              QKC_[r, h // 2, NP:T], True, True)
                last.then_inc(s_sintra, 1)
                wait(t["sw"])
                wait(c0)
                for h in range(HC):
                    mm(TB[:, 0, h * NS:(h + 1) * NS], TV2[0:NS, TILES, h * P:(h + 1) * P], WSM[0:NS, h, :],
                       h == 0, False)
                mm(TB[:, 1, 0:HC * NS], ones[0:NS, :], WSM[0:NS, :, :], True, False)
                mm(TB[:, 1, 0:HC * NS], ones, QN, False, True)
                for hp in range(2):
                    for s in range(SEQS):
                        o = TB[:, 0, 2 * hp * NS:2 * (hp + 1) * NS].rearrange("p (h n) -> p h n", h=2)
                        last = mm(o[:, :, s * STEPS:(s + 1) * STEPS], CS[:, hp, s, :],
                                  QW[:, hp, :, s * STEPS:(s + 1) * STEPS], False, hp == 1 and s == SEQS - 1)
                last.then_inc(s_num, 1)
                wait(t["kws"])
                for hp in range(2):
                    p = unit()
                    for h2 in range(2):
                        wait(t["vblk"])
                        h = 2 * hp + h2
                        for sh in range(2):
                            last = mm(G[64 * h2:64 * h2 + 64, 2 * p + sh, :], KCT[0:NS, TILES, h * 64:(h + 1) * 64],
                                      VBLK[0:NS, h2, 4 * sh:4 * sh + 4, :], True, True)
                    last.then_inc(s_unit, 1)
                p = unit()
                for hp in range(2):
                    last = mm(G[:, 2 * p, hp * SEQS:(hp + 1) * SEQS], KCT[0:NS, TILES, hp * P:(hp + 1) * P], own_seq,
                              True, True)
                last.then_inc(s_unit, 1)
                project(4)
                project(4)
                project_tokens()
                for m in range(8):
                    wait(t["sqn"])
                    product(unit(), [halfones], lambda k: SQ[:, m % 2, :])
                wait(t["qkr"], 8)
                for hp in range(4):
                    for h in (2 * hp, 2 * hp + 1):
                        product(unit(), [sel_neg[:, h, :]], lambda k: ROWA[0:ROWS, :])
                    pair = unit()
                    todo = [(h, i) for h in (2 * hp, 2 * hp + 1) for i in range(TILES)]

                    def scores(n):
                        h, i = todo[n]
                        r = slice(64 * (h % 2), 64 * (h % 2) + 64)
                        it = hp * 8 + n
                        if it >= 2:
                            wait(t["mx"])
                        mm(Q[:, it % 2, 0:(i + 1) * P], QKB[r, hp, i * P:(i + 1) * P], QKB[r, 4 + hp, 0:(i + 1) * P],
                           True, False)
                        mm(Q[:, it % 2, i * P:(i + 1) * P], ident, earlier, False, True).then_inc(s_sc, 1)

                    def turns(n):
                        h, i = todo[n]
                        it = hp * 8 + n
                        wait(t["p"])
                        for j in range(i + 1):
                            last = turn(TB[:, it % 2, j * P:(j + 1) * P], SCR[:, it % 2, j * P:(j + 1) * P], ident)
                        last.then_inc(s_pt, 1)

                    def values(n):
                        h, i = todo[n]
                        it = hp * 8 + n
                        wait(t["ptc"])
                        r = slice(64 * (h % 2), 64 * (h % 2) + 64)
                        for j in range(i + 1):
                            last = mm(G[r, 2 * pair, i * P:(i + 1) * P], TV2[:, j, h * 64:(h + 1) * 64],
                                      SCR[:, 2 + it % 2, j * P:(j + 1) * P], j == 0, j == i)
                        if n == 7:
                            last.then_inc(s_unit, 1)

                    for n in range(8 + 2):
                        if n < 8:
                            scores(n)
                        if 1 <= n <= 8:
                            turns(n - 1)
                        if n >= 2:
                            values(n - 2)
                wait(t["mx"], 2)
                wait(t["qs"])
                pe.sem_inc(s_pgu, 4)
                for g in range(2):
                    wait(t["ln"])
                    p = unit()
                    mm(G[:, 2 * p, 0:NS], DIAG[0:NS, g, :], seq01, True, True).then_inc(s_unit, 1)
                for g in range(2):
                    if g == 1:
                        wait(t["smx"])
                    for s in range(4):
                        r = slice(32 * s, 32 * s + 32)
                        for pg in range(PAGES):
                            wait(pin_sp[pg // 2] if g and pg % 2 else pin[pg])
                            for hp in range(4):
                                last = mm(Q[r, pg // 4, (pg % 4) * P:(pg % 4 + 1) * P],
                                          QS[:, hp, 4 * g + s, :, :], PLACES[pg][:, hp * P:(hp + 1) * P],
                                          hp == 0, hp == 3)
                            last.then_inc(s_pgu, 1)
                        for hp in range(4):
                            last = mm(TB[r, 0, 0:NS], QS[:, hp, 4 * g + s, :, :], QKB[:, 4 + hp, NP:T],
                                      hp == 0, hp == 3)
                    last.then_inc(s_ss, 1)
                for g in range(2):
                    wait(t["ps"])
                    p = unit()
                    for pg in range(PAGES):
                        last = turn(G[:, 2 * p + pg // 4, (pg % 4) * P:(pg % 4 + 1) * P],
                                    SSC[:, pg * P:(pg + 1) * P], ident)
                    last.then_inc(s_unit, 1)
                    p = unit()
                    apart(pe)
                    turn(G[0:NS, 2 * p, 0:P], SSC[:, PAST:PAST + NS], ident).then_inc(s_unit, 1)
                    for q in range(2):
                        pe.wait_ge(s_dr[q], un.d[q].value())
                    if g == 1:
                        wait(t["pvc"])
                    for s in range(4):
                        for pg in range(PAGES):
                            wait(pin[pg])
                            for hp in range(4):
                                last = mm(TB[:, 1, (s * 4 + hp) * 8:(s * 4 + hp + 1) * 8],
                                          PLACES[pg][:, hp * P:(hp + 1) * P],
                                          PT[:, pg, s * 32 + hp * 8:s * 32 + hp * 8 + 8],
                                          s + pg + hp == 0, False)
                            last.then_inc(s_pgu, 1)
                    for s in range(4):
                        for hp in range(4):
                            last = mm(TB[:, 1, (s * 4 + hp) * 8:(s * 4 + hp + 1) * 8],
                                      TV2[0:NS, TILES, hp * P:(hp + 1) * P],
                                      PT[0:NS, 8, s * 32 + hp * 8:s * 32 + hp * 8 + 8], False, s + hp == 6)
                    last.then_inc(s_pv, 1)
                wait(t["pvc"])
                wait(t["smx"])
                apart(pe)
                with repeat(pe, KD, un.strides(6) | {w_in[0]: 1, w_in[1]: 1}):
                    s = weights()
                    for b in range(3):
                        product(unit(), [W[s][:, (k * 3 + b) * P:(k * 3 + b + 1) * P] for k in range(KD)], hk)
                    s = weights()
                    for b in range(3):
                        product(unit(), [W[s][:, (b * 4 + k) * P:(b * 4 + k + 1) * P] for k in range(4)],
                                lambda k: YS[:, b, k, :])
                wait(t["m"], KD)
                apart(pe)
                with repeat(pe, OUT_STEPS // 2, un.strides(8) | {w_in[0]: 1, w_in[1]: 1}):
                    for _ in range(2):
                        s = weights()
                        w = W[s][:, :].rearrange("p (k n) -> p k n", k=KD)
                        for b in range(4):
                            product(unit(), [w[:, k, b * P:(b + 1) * P] for k in range(KD)], lambda k: MT[:, k, :])
                norm_sums()
                ffn()

        @block.scalar
        def _(ac):
            un = Units()
            small = Tally(s_small, 16)
            t = {k: Tally(s) for k, s in dict(xup=s_xup, vardy=s_vardy, x1=s_x1, rowd=s_rowd, rows=s_rows,
                                              wrow=s_wrow, diag=s_diag, wt=s_wt, yc=s_yc, sarg=s_sarg, qkr=s_qkr,
                                              mx=s_max, p=s_p, pt=s_pt, smx=s_smx, stn=s_stn).items()}
            t["tn"] = Tally(s_tn)
            mr = Tally(s_mr)
            w_in = [Tally(s_w[0], 16), Tally(s_w[1], 16)]
            st = Tally(s_ac)
            outs = Tally(s_outa, 16)
            outa = d["outs"]

            def wait(tally, n=1):
                tally.n += n
                ac.wait_ge(tally.sem, tally.value())

            def link(ins):
                st.n += 1
                ins.then_inc(s_ac, 1)
                ac.wait_ge(s_ac, st.value())

            def mine():
                p = un.take()
                ac.wait_ge(s_unit, un.u.value())
                return p

            def both(p, m=P):
                return G[0:m, 2 * p:2 * p + 2, 0:HALF]

            def drained(ins, p):
                ins.then_inc(s_dr[p], 1)

            def store(dst, src):
                outs.n += 1
                ac.dma_start(dst, src).then_inc(s_outa, 16)

            def norm(before_root=None):
                for k in range(KD):
                    wait(t["xup"])
                    ac.activation(H[:, k, :], X[:, k, :], ACT.Square).then_inc(s_sq, 1)
                if before_root:
                    before_root()
                p = mine()
                ac.activation(halves(RS), both(p), ACT.Sqrt, bias=EPSC[:, 0:1], scale=1.0 / D).then_inc(s_rms, 1)

            def ffn(base):
                plan, at = ffn_plan(), [0]

                def split():
                    i = at[0]
                    at[0] += 1
                    step, o, n = plan[i]
                    slot = (base + step) % 2
                    if i == 0 or plan[i - 1][0] != step:
                        wait(w_in[slot])
                    ac.activation(WH[i % 2][:, 0:n], W[slot][:, o:o + n], ACT.Copy).then_inc(s_wh, 1)

                def first_splits():
                    ac.wait_ge(s_unit, un.u.value())
                    split()
                    split()

                def chunk(c):
                    p = mine()
                    split()
                    drained(ac.activation(halves(SIL[:, c % 2, :]), both(p), ACT.Silu, bias=ZERO[:, 0:1]), p)
                    mine()
                    split()

                norm(first_splits)
                for k in range(KD):
                    wait(t["tn"])
                    ac.activation(HH[:, k, :], TN[:, k % 2, :], ACT.Copy).then_inc(s_hh, 1)
                for blocks in FF_PART:
                    with repeat(ac, 2, un.strides(8) | {w_in[0]: 1, w_in[1]: 1}):
                        for c in range(4):
                            chunk(c)
                    at[0] += 8
                    for c in range(blocks - 8):
                        chunk(c)
                    for _ in range(KD):
                        mine()
                        if at[0] < len(plan):
                            split()

            def pass_steps(first, n):
                for i in range(n):
                    w_in[(first + i) % 2].n += 1

            def each(n, f):
                for i in range(n):
                    p = mine()
                    drained(f(i, p), p)

            def tokens(dst, func):
                def f(i, p):
                    m = P if i < TILES else NS
                    return ac.activation(dst[0:m, i, :], G[0:m, 2 * p, :], func, **({} if func == ACT.Copy else
                                                                                  dict(bias=ZERO[0:m, 0:1])))
                each(5, f)

            ac.wait_ge(s_in, 64)
            ac.wait_ge(s_eps, 1)
            ac.activation(COND[:], COND[:], ACT.Silu, bias=ZERO[:, 0:1]).then_inc(s_cond, 1)
            ac.wait_ge(s_cond, 1)
            ac.activation(CHL[:, :, 0:C], COND[:], ACT.Copy).then_inc(s_cond, 1)
            strides = un.layer() | {st: 3, t["xup"]: 24, t["vardy"]: 5, t["x1"]: 1, t["rowd"]: 1, t["rows"]: 1,
                                    t["wrow"]: 1, t["diag"]: 16, t["wt"]: 16, t["yc"]: 5, t["sarg"]: 1,
                                    t["qkr"]: 8, t["mx"]: 32, t["p"]: 32, t["pt"]: 32, t["smx"]: 2, t["stn"]: 4,
                                    outs: 11, small: 11, t["tn"]: 2 * KD, mr: ADA_STEPS,
                                    w_in[0]: STEPS_L // 2, w_in[1]: STEPS_L // 2}
            with repeat(ac, L, strides) as l:
                lay = bass.ds(l, 1)
                ac.wait_ge(s_unit, un.u.value())
                def split(s):
                    wait(w_in[s])
                    ac.activation(WHA[s][:], W[s][:], ACT.Copy).then_inc(s_wh, 1)

                def rows(s):
                    p = mine()
                    ac.activation(MR[0:2 * C, s, :], G[0:2 * C, 2 * p, :], ACT.Copy).then_inc(s_mr, 1)
                    mr.n += 1
                    ac.wait_ge(s_mr, mr.value())
                    ac.sem_inc(s_dr[p], 1)

                split(0)
                split(1)
                rows(0)
                with repeat(ac, ADA_STEPS // 2 - 1, un.strides(4) | {w_in[0]: 1, w_in[1]: 1, mr: 2}):
                    for s in range(2):
                        split(s)
                        rows(1 - s)
                        un.take()
                rows(1)
                un.take(2)
                ffn(ADA_STEPS)
                norm()
                each(4, lambda i, p: ac.activation(halves(YA[:, i, :]), both(p), ACT.Gelu_apprx_tanh,
                                                   bias=ZERO[:, 0:1]))
                tokens(TV, ACT.Gelu_apprx_tanh)
                for q in range(2):
                    ac.wait_ge(s_dr[q], un.d[q].value())
                for i in range(5):
                    m = P if i < TILES else NS
                    last = ac.activation(SCR[0:m, i, :], TV[0:m, i, :], ACT.Square, accum_out=SMALL[0:m, i:i + 1])
                link(last)
                for i in range(5):
                    m = P if i < TILES else NS
                    ac.activation(SMALL[0:m, 8 + i:9 + i], SMALL[0:m, i:i + 1], ACT.Sqrt, bias=EPSC[0:m, 0:1],
                                  scale=1.0 / 512).then_inc(s_vrms, 1)
                wait(t["vardy"], 5)
                store(outa["chunk_v"][lay].rearrange("a p n -> (a p) n"), TV[0:NS, TILES, :])
                un.take(4)
                each(4, lambda i, p: ac.activation(halves(QKC_[:, i, :]), both(p), ACT.Copy,
                                                   scale=1.0 if i < 2 else DKC ** -0.5))
                tokens(TV2, ACT.Copy)
                each(4, lambda i, p: ac.activation(halves(YC[:, i, :]), both(p), ACT.Sigmoid, bias=ZERO[:, 0:1]))
                un.take()
                wait(t["x1"])
                link(ac.activation(ROWM[0:ROWS], ROWF[0:ROWS], ACT.Abs, bias=ZERO[0:ROWS, 0:1]))
                link(ac.activation(ROWM[0:ROWS], ROWM[0:ROWS], ACT.Exp, bias=ZERO[0:ROWS, 0:1], scale=-1.0))
                ac.activation(ROWM[0:ROWS], ROWM[0:ROWS], ACT.Ln, bias=ones[0:ROWS, 0:1]).then_inc(s_sp, 1)
                wait(t["rowd"])
                store(outa["logf"][lay].rearrange("a h n -> (a h) n"), ROWF[0:HB, :])
                each(5, lambda i, p: ac.activation(KCT[0:P if i < TILES else NS, i, :],
                                                   G[0:P if i < TILES else NS, 2 * p, 0:256], ACT.Copy))
                wait(t["rows"])
                store(outa["m"][lay].rearrange("a h n -> (a h) n"), ROWM[HB:ROWS, NP - 1:T])
                wait(t["wrow"])
                ac.activation(SROW[0:ROWS, 0:2, :], SROW[0:ROWS, 0:2, :], ACT.Exp, bias=ZERO[0:ROWS, 0:1])\
                    .then_inc(s_exr, 1)
                un.take()
                each(4, lambda i, p: ac.activation(halves(GB[:, i, :]), both(p), ACT.Copy))
                un.take()
                for q in range(2):
                    ac.wait_ge(s_dr[q], un.d[q].value())
                for h in range(HC):
                    last = ac.activation(WKC[:, h, :], COL[:, 0:48].rearrange("p (i r) -> p i r", r=12)[:, :, HB + h],
                                         ACT.Exp, bias=GB[:, h, NP - 1:NP])
                last.then_inc(s_wkc, 1)
                for h in range(HC):
                    p = mine()
                    if h >= 2:
                        wait(t["yc"])
                    ac.activation(EM[:, h % 2, 0:HALF], G[:, 2 * p, 0:HALF], ACT.Exp, bias=ZERO[:, 0:1])
                    ac.activation(EM[:, h % 2, HALF:NP], G[:, 2 * p + 1, 0:NP - HALF], ACT.Exp,
                                  bias=ZERO[:, 0:1])
                    drained(ac.activation(EMS[:, h, :], G[:, 2 * p + 1, NP - HALF:HALF], ACT.Exp,
                                          bias=ZERO[:, 0:1]), p)
                    for j in range(TILES):
                        n = h * TILES + j
                        a = COL[:, j * 12 + HB + h:j * 12 + HB + h + 1]
                        wait(t["diag"])
                        if n >= 2:
                            wait(t["wt"])
                        e = SCR[:, n % 2, :]
                        last = ac.activation(e[:, j * P:(j + 1) * P], DIAG[:, n % 2, :], ACT.Exp, bias=a)
                        if j < TILES - 1:
                            last = ac.activation(e[:, (j + 1) * P:NP], GB[:, h, (j + 1) * P:NP], ACT.Exp, bias=a)
                        last.then_inc(s_e, 1)
                    un.take()
                wait(t["wt"], 2)
                wait(t["yc"], 2)
                un.take()
                wait(t["stn"])
                store(outa["C_prompt"][lay].rearrange("a p h v -> (a p) h v"),
                      EM[:, 0, 0:256].rearrange("p (h v) -> p h v", h=2))
                store(outa["n_prompt"][lay].rearrange("a p h -> (a p) h"), EM[:, 1, 0:2])
                wait(t["sarg"])
                for h in range(HC):
                    last = ac.activation(ES[0:NS, h, :], ARG[0:NS, h, :], ACT.Exp,
                                         bias=COL[0:NS, 48 + HB + h:49 + HB + h])
                last.then_inc(s_ses, 1)
                for hp in range(2):
                    un.take()
                    wait(t["stn"])
                    store(outa["C_sample"][lay, hp].rearrange("a p s v -> (a p) s v"), CS[:, hp, :, :])
                un.take()
                wait(t["stn"])
                store(outa["n_sample"][lay].rearrange("a p h s -> (a p) h s"), N0[:])
                wait(t["yc"])
                ac.wait_ge(s_outa, outs.value())
                each(8, lambda i, p: ac.activation(halves(QKB[:, i, :]), both(p), ACT.Copy))
                tokens(TV2, ACT.Copy)
                for q in range(2):
                    ac.wait_ge(s_dr[q], un.d[q].value())
                store(outa["v"][lay, 0:NP].rearrange("a (i p) n -> p (a i) n", p=P), TV2[:, 0:TILES, :])
                store(outa["v"][lay, NP:T].rearrange("a p n -> (a p) n"), TV2[0:NS, TILES, :])
                for m in range(8):
                    ac.activation(SQ[:, m % 2, :], QKB[:, m, :], ACT.Square).then_inc(s_sqn, 1)
                    p = mine()
                    if m >= 2:
                        wait(t["qkr"])
                    ac.activation(halves(RT[:, m % 2, :]), both(p), ACT.Sqrt,
                                  bias=EPSC[:, 1:2] if m < 4 else EPSC[:, 0:1],
                                  scale=1.0 if m < 4 else 1.0 / DB).then_inc(s_rtn, 1)
                wait(t["qkr"], 2)
                store(outa["k"][lay].rearrange("a p m n -> (a p) m n"), QKB[:, 4:8, :])
                for hp in range(4):
                    for h2 in range(2):
                        h = 2 * hp + h2
                        p = mine()
                        last = ac.activation(NF[:, h % 4, 0:HALF], G[:, 2 * p, 0:HALF], ACT.Copy)
                        last = ac.activation(NF[:, h % 4, HALF:NP], G[:, 2 * p + 1, 0:NP - HALF], ACT.Copy)
                        drained(last, p)
                    for n in range(8):
                        it, i = hp * 8 + n, n % TILES
                        w = (i + 1) * P
                        wait(t["mx"])
                        ac.activation(SCR[:, it % 2, 0:w], SCR[:, it % 2, 0:w], ACT.Exp,
                                      bias=SMALL[:, 16 + it % 2:17 + it % 2],
                                      accum_out=SMALL[:, 20 + it % 2:21 + it % 2]).then_inc(s_exp, 1)
                        if n >= 1:
                            wait(t["pt"])
                            w = ((n - 1) % TILES + 1) * P
                            ac.activation(SCR[:, 2 + (it - 1) % 2, 0:w], TB[:, (it - 1) % 2, 0:w],
                                          ACT.Copy).then_inc(s_ptc, 1)
                    wait(t["pt"])
                    ac.activation(SCR[:, 2 + it % 2, 0:NP], TB[:, it % 2, :], ACT.Copy).then_inc(s_ptc, 1)
                    p = mine()
                    drained(ac.activation(YB[:, hp, 0:NP], G[:, 2 * p, :], ACT.Copy), p)
                wait(t["p"], 32)
                un.take(2)
                for g in range(2):
                    wait(t["smx"])
                    ac.activation(SSC, SSC, ACT.Exp, bias=SMALL[:, 24:25], accum_out=SMALL[:, 25:26])\
                        .then_inc(s_sex, 1)
                    p = mine()
                    drained(ac.activation(PT[:, 0:8, :].rearrange("p (a b) n -> p a (b n)", a=2),
                                          G[:, 2 * p:2 * p + 2, :], ACT.Copy), p)
                    p = mine()
                    drained(ac.activation(PT[0:NS, 8, :], G[0:NS, 2 * p, 0:P], ACT.Copy), p)
                ac.wait_ge(s_outa, outs.value())
                with repeat(ac, KD, un.strides(6)):
                    for b in range(3):
                        p = mine()
                        drained(ac.activation(halves(GT[:, b, :]), both(p), ACT.Sigmoid, bias=ZERO[:, 0:1]), p)
                    un.take(3)
                un.take(KD)
                mixer_steps = STEPS_L - ADA_STEPS - 2 * FFN_STEPS
                pass_steps(ADA_STEPS + FFN_STEPS, mixer_steps)
                ffn(ADA_STEPS + FFN_STEPS + mixer_steps)
                wait(small, 11)
            ac.wait_ge(s_outa, outs.value())

        @block.vector
        def _(ve):
            un = Units()
            small = Tally(s_small, 16)
            t = {k: Tally(s) for k, s in dict(rms=s_rms, vrms=s_vrms, sp=s_sp, e=s_e, wkc=s_wkc, rowd=s_rowd, qkr=s_qkr, m=s_m,
                                              sintra=s_sintra, ses=s_ses, num=s_num, qk=s_qk, rtn=s_rtn, sc=s_sc,
                                              exp=s_exp, pt=s_pt, sex=s_sex, ss=s_ss, pv=s_pv,
                                              ).items()}
            lf = Tally(s_lf, 16)
            c0 = Tally(s_c0, 16)
            st = Tally(s_dv)
            wh, hh, hr, acts = Tally(s_wh), Tally(s_hh), Tally(s_h), Tally(s_acts)

            def wait(tally, n=1):
                tally.n += n
                ve.wait_ge(tally.sem, tally.value())

            def link(ins):
                st.n += 1
                ins.then_inc(s_dv, 1)
                ve.wait_ge(s_dv, st.value())

            def mine():
                p = un.take()
                ve.wait_ge(s_unit, un.u.value())
                return p

            def both(p, m=P):
                return G[0:m, 2 * p:2 * p + 2, 0:HALF]

            def drained(ins, p):
                ins.then_inc(s_dr[p], 1)

            def by_seq(x):
                return x.rearrange("p (s t) -> p s t", t=STEPS)

            def norm(part):
                p = mine()
                wait(t["rms"])
                drained(ve.reciprocal(RS, RS), p)
                ve.wait_ge(s_dr[p], un.d[p].value())
                for k in range(KD + 1):
                    if k < KD:
                        split = part != 1
                        o = TN[:, k % 2, :] if split else H[:, k, :]
                        if split and k >= 2:
                            ve.wait_ge(s_h, hr.value())
                        link(ve.tensor_tensor(o, X[:, k, :], RS, ALU.mult))
                        ve.tensor_scalar(o[:, 0:NP], o[:, 0:NP], AMP[:, part, k, 0:1],
                                         MOD[:, part * 24 + k, 0:1], ALU.mult, ALU.add)
                        hs = by_seq(o[:, NP:T])
                        link(ve.tensor_tensor(hs, hs, AMP[:, part, k, 1:C][:, :, None]
                                              .to_broadcast([P, SEQS, STEPS]), ALU.mult))
                        ve.tensor_tensor(hs, hs, MOD[:, part * 24 + k, 1:C][:, :, None]
                                         .to_broadcast([P, SEQS, STEPS]), ALU.add).then_inc(s_tn if split else s_h, 1)
                        if not split:
                            hr.n += 1
                    if split and k >= 1:
                        wait(hh)
                        ve.tensor_tensor(HL[:, k - 1, :], TN[:, (k - 1) % 2, :], HH[:, k - 1, :], ALU.subtract)\
                            .then_inc(s_h, 1)
                        hr.n += 1

            def ffn(part, base):
                plan, at = ffn_plan(), [0]

                def split():
                    i = at[0]
                    at[0] += 1
                    step, o, n = plan[i]
                    wait(wh)
                    ve.tensor_tensor(WL[i % 2][:, 0:n], W[(base + step) % 2][:, o:o + n], WH[i % 2][:, 0:n],
                                     ALU.subtract).then_inc(s_wl, 1)

                def chunk(c, m):
                    q = un.take()
                    split()
                    p = mine()
                    ve.wait_ge(s_dr[q], un.d[q].value())
                    drained(ve.tensor_tensor(halves(PR), halves(SIL[:, c % 2, :]), both(p), ALU.mult), p)
                    ve.wait_ge(s_dr[p], un.d[p].value())
                    link(ve.tensor_copy(AH[:, m, :], PR))
                    ve.tensor_tensor(AL[:, m, :], PR, AH[:, m, :], ALU.subtract).then_inc(s_acts, 1)
                    wait(acts)
                    split()

                split()
                split()
                norm(part)
                for half, blocks in enumerate(FF_PART):
                    with repeat(ve, 2, un.strides(8) | {wh: 8, st: 4, acts: 4}) as i:
                        for c in range(4):
                            chunk(c, i * 4 + c)
                    at[0] += 8
                    for c in range(8, blocks):
                        chunk(c, c)
                    for m in range(KD):
                        p = mine()
                        add_block(X[:, m, :], MOD[:, part * 24 + 16 + m, :], p, m % 2, half == 1)
                        if at[0] < len(plan):
                            split()

            def add_block(xb, gb, p, j, done):
                ve.scalar_tensor_tensor(xb[:, 0:HALF], G[:, 2 * p, 0:HALF], gb[:, 0:1], xb[:, 0:HALF],
                                        ALU.mult, ALU.add)
                ve.scalar_tensor_tensor(xb[:, HALF:NP], G[:, 2 * p + 1, 0:NP - HALF], gb[:, 0:1],
                                        xb[:, HALF:NP], ALU.mult, ALU.add)
                tmp = TMP[:, j, :]
                ve.tensor_tensor(by_seq(tmp), by_seq(G[:, 2 * p + 1, NP - HALF:HALF]),
                                 gb[:, 1:C][:, :, None].to_broadcast([P, SEQS, STEPS]), ALU.mult)\
                    .then_inc(s_dv, 1)
                st.n += 1
                ve.wait_ge(s_dv, st.value())
                ve.sem_inc(s_dr[p], 1)
                last = ve.tensor_tensor(xb[:, NP:T], xb[:, NP:T], tmp, ALU.add)
                if done:
                    last.then_inc(s_xup, 1)
                else:
                    link(last)

            def add_to_x(gate):
                with repeat(ve, KD // 2, un.strides(2) | {st: 2}) as i:
                    for j in range(2):
                        p = mine()
                        add_block(X[:, bass.ds(i * 2 + j, 1), :].rearrange("p a n -> p (a n)"),
                                  MOD[:, bass.ds(i * 2 + (gate + j), 1), :].rearrange("p a n -> p (a n)"), p, j, True)

            ve.memset(EPSC[:, 0:1], EPS)
            ve.memset(EPSC[:, 1:2], DB * EPS)
            ve.memset(ZERO[:], 0.0).then_inc(s_eps, 1)
            ve.memset(QS[:], 0.0)
            ve.memset(QW[:], 0.0).then_inc(s_zero, 1)
            ve.wait_ge(s_zero, 1)
            ve.sem_inc(s_unit, 2)
            ve.sem_inc(s_dr[0], 1)
            ve.sem_inc(s_dr[1], 1)
            ve.sem_inc(s_pgu, 4)
            ve.sem_inc(s_smallf, 1)
            ve.sem_inc(s_xup, KD)
            ve.wait_ge(s_in, 64)
            strides = un.layer() | {st: VE_LINKS, t["rms"]: 3, t["vrms"]: 5, t["sp"]: 1, t["e"]: 16, t["rowd"]: 1, t["qkr"]: 8, t["m"]: KD,
                                    t["wkc"]: 1, t["sintra"]: 1, t["ses"]: 1, t["num"]: 1, t["qk"]: 16,
                                    t["rtn"]: 8, t["sc"]: 32, t["exp"]: 32, t["pt"]: 32, t["sex"]: 2, t["ss"]: 2,
                                    t["pv"]: 2, small: 11, lf: 64, c0: 1,
                                    wh: ADA_STEPS + 2 * len(ffn_plan()), hh: 2 * KD, hr: 3 * KD, acts: 2 * KF}
            ve.wait_ge(s_cond, 2)
            ve.tensor_tensor(CHL[:, :, C:2 * C], COND[:], CHL[:, :, 0:C], ALU.subtract).then_inc(s_cond, 1)
            with repeat(ve, L, strides):
                wait(small, 11)
                apart(ve)
                def split_step(j):
                    wait(wh)
                    ve.tensor_tensor(WLA[j][:], W[j][:], WHA[j][:], ALU.subtract).then_inc(s_wl, 1)

                def biased(at4):
                    p = mine()
                    drained(ve.tensor_tensor(MOD[:, at4, :], G[:, 2 * p, 0:4 * C].rearrange("p (b c) -> p b c", b=4),
                                             BADA[:, at4][:, :, None].to_broadcast([P, 4, C]), ALU.add), p)

                split_step(0)
                split_step(1)
                un.take()
                with repeat(ve, ADA_STEPS // 2 - 1, un.strides(4) | {wh: 2}) as i:
                    for j in range(2):
                        split_step(j)
                        un.take()
                        biased(bass.ds(i * 8 + 4 * j, 4))
                un.take()
                for j in range(2):
                    biased(slice(9 * KD - 8 + 4 * j, 9 * KD - 4 + 4 * j))
                for q in range(2):
                    ve.wait_ge(s_dr[q], un.d[q].value())
                for part in range(3):
                    o = part * 24
                    last = ve.scalar_tensor_tensor(AMP[:, part], MOD[:, o + 8:o + 16, :], 1.0,
                                                   GN[:, part, :][:, :, None].to_broadcast([P, KD, C]),
                                                   ALU.add, ALU.mult)
                    if part != 1:
                        last = ve.tensor_scalar(MOD[:, o + 16:o + 24, :], MOD[:, o + 16:o + 24, :], 0.5, None, ALU.mult)
                link(last)
                ffn(0, ADA_STEPS)
                norm(1)
                ve.tensor_tensor(WST[:], WST[:], tril01[:, None, :].to_broadcast([P, 4, P]), ALU.mult).then_inc(s_ws, 1)
                ve.tensor_tensor(WSS[:], WSS[:], seq01[:, None, :].to_broadcast([NS, 4, NS]), ALU.mult).then_inc(s_ws, 1)
                un.take(9)
                for i in range(5):
                    m = P if i < TILES else NS
                    wait(t["vrms"])
                    r = SMALL[0:m, 8 + i:9 + i]
                    link(ve.reciprocal(r, r))
                    ve.scalar_tensor_tensor(TV[0:m, i, :], TV[0:m, i, :], r, GVA[0:m, :], ALU.mult, ALU.mult)\
                        .then_inc(s_vardy, 1)
                for g in range(4):
                    p = mine()
                    a = SCR[:, 6, :].rearrange("p (n t) -> p n t", n=TILES)
                    b = TMP[:, g % 2, :]
                    ve.tensor_tensor(a, G[:, 2 * p, :].rearrange("p (n t) -> p n t", n=TILES),
                                     BS[:, g, :][:, None, :].to_broadcast([P, TILES, P]), ALU.add)
                    drained(ve.tensor_tensor(by_seq(b), by_seq(G[:, 2 * p + 1, 0:NS]),
                                             BS[:, g, 0:STEPS][:, None, :].to_broadcast([P, SEQS, STEPS]), ALU.add), p)
                    ve.wait_ge(s_dr[p], un.d[p].value())
                    ve.tensor_tensor(YA[:, g, 0:NP], YA[:, g, 0:NP], SCR[:, 6, :], ALU.mult)
                    last = ve.tensor_tensor(YA[:, g, NP:T], YA[:, g, NP:T], b, ALU.mult)
                    if g < 3:
                        link(last)
                    else:
                        last.then_inc(s_c0f, 1)
                un.take(13)
                p = mine()
                ve.tensor_scalar(halves(ROWF[0:ROWS]), both(p, ROWS), BROWS[0:ROWS, 0:1], None, ALU.add).then_inc(s_x1, 1)
                drained(ve.tensor_scalar(halves(ROWA[0:ROWS]), G[32:32 + ROWS, 2 * p:2 * p + 2, 0:HALF],
                                         BROWS[32:32 + ROWS, 0:1], None, ALU.add), p)
                ve.wait_ge(s_dr[p], un.d[p].value())
                F_, A_, M_, G_ = ROWF[0:ROWS], ROWA[0:ROWS], ROWM[0:ROWS], ROWG[0:ROWS]

                def step_of(x, k):
                    return x[:, NP + k:T:STEPS]

                wait(t["sp"])
                ve.scalar_tensor_tensor(F_, F_, 0.0, M_, ALU.min, ALU.subtract).then_inc(s_rowd, 1)
                wait(t["rowd"])
                link(ve.tensor_tensor_scan(M_[:, 0:NP], ones[0:ROWS, 0:1].to_broadcast([ROWS, NP]), F_[:, 0:NP], 0.0,
                                           ALU.mult, ALU.add))
                link(ve.tensor_copy(step_of(M_, 0), step_of(F_, 0)))
                for k in range(1, STEPS):
                    link(ve.tensor_tensor(step_of(M_, k), step_of(M_, k - 1), step_of(F_, k), ALU.add))
                link(ve.tensor_tensor(A_, A_, M_, ALU.subtract))
                link(ve.tensor_tensor_scan(G_[:, 0:NP], A_[:, 0:NP], A_[:, 0:NP], 0.0, ALU.max, ALU.max))
                link(ve.tensor_tensor(step_of(G_, 0), M0[:], step_of(A_, 0), ALU.max))
                for k in range(1, STEPS):
                    link(ve.tensor_tensor(step_of(G_, k), step_of(G_, k - 1), step_of(A_, k), ALU.max))
                ve.tensor_tensor(M_, M_, G_, ALU.add).then_inc(s_rows, 1)
                ve.tensor_tensor(by_seq(SROW[0:ROWS, 0, :]), M0[:][:, :, None].to_broadcast([ROWS, SEQS, STEPS]),
                                 by_seq(G_[:, NP:T]), ALU.subtract)
                ve.tensor_tensor(by_seq(SROW[0:ROWS, 1, :]), by_seq(A_[:, NP:T]),
                                 step_of(G_, STEPS - 1)[:, :, None].to_broadcast([ROWS, SEQS, STEPS]), ALU.subtract)\
                    .then_inc(s_wrow, 1)
                un.take(5)
                p = mine()
                ve.tensor_copy(COL[:, 0:48], G[:, 2 * p, 0:48])
                drained(ve.tensor_copy(COL[0:NS, 48:84], G[0:NS, 2 * p, 48:84]), p)
                un.take(4)
                p = mine()
                drained(ve.tensor_copy(WIB, G[:, 2 * p, 0:2 * NS].rearrange("p (h n) -> p h n", h=2)), p)
                for q in range(2):
                    ve.wait_ge(s_dr[q], un.d[q].value())
                def diag(n):
                    h, j = divmod(n, TILES)
                    ve.tensor_tensor(DIAG[:, n % 2, :], GB[:, h, j * P:(j + 1) * P], later, ALU.add).then_inc(s_diag, 1)

                diag(0)
                for h in range(HC):
                    q = un.take()
                    for j in range(TILES):
                        n = h * TILES + j
                        if n + 1 < HC * TILES:
                            diag(n + 1)
                        wait(t["e"])
                        wait(t["qk"])
                        ve.tensor_tensor(SCR[:, 2 + n % 2, j * P:NP], SCR[:, n % 2, j * P:NP], Q[:, n % 2, j * P:NP],
                                         ALU.mult).then_inc(s_wt, 1)
                    p = mine()
                    ve.wait_ge(s_dr[q], un.d[q].value())
                    d_ = SCR[:, 4, :]
                    link(ve.scalar_tensor_tensor(d_, G[:, 2 * p + 1, :], -1.0, EM[:, h % 2, :], ALU.mult, ALU.max))
                    link(ve.tensor_tensor(d_, d_, G[:, 2 * p + 1, :], ALU.max))
                    link(ve.reciprocal(d_, d_))
                    ve.tensor_tensor(SCR[:, 5, :], G[:, 2 * p, :], d_, ALU.mult).then_inc(s_dr[p], 1)
                    ve.wait_ge(s_dr[p], un.d[p].value())
                    ve.tensor_tensor(YC[:, h, 0:NP], YC[:, h, 0:NP], SCR[:, 5, :], ALU.mult).then_inc(s_yc, 1)
                wait(t["wkc"])
                for i in range(TILES):
                    kt = KCT[:, i, :].rearrange("p (h d) -> p h d", h=HC)
                    last = ve.tensor_tensor(kt, kt, WKC[:, :, i:i + 1].to_broadcast([P, HC, DKC]), ALU.mult)
                last.then_inc(s_kw, 1)
                p = mine()
                ve.tensor_copy(EM[:, 0, 0:256], G[:, 2 * p, 0:256])
                ve.tensor_copy(EM[:, 1, 0:2], G[:, 2 * p + 1, 0:2]).then_inc(s_dr[p], 1)
                ve.wait_ge(s_dr[p], un.d[p].value())
                ve.sem_inc(s_stn, 1)
                ve.tensor_tensor(ARG[0:NS], GB[0:NS, :, NP:T], seq_later[:, None, :].to_broadcast([NS, HC, NS]),
                                 ALU.add).then_inc(s_sarg, 1)
                for hp in range(2):
                    for h2 in range(2):
                        r = slice(64 * h2, 64 * h2 + 64)
                        last = ve.tensor_tensor(QW[r, hp, h2, :], QKC_[r, hp, NP:T], WIB[r, hp, :], ALU.mult)
                link(last)
                for hp in range(2):
                    for h2 in range(2):
                        last = ve.tensor_tensor(by_seq(QN[:, hp, h2, :]), by_seq(QW[:, hp, h2, :]),
                                                N0[:, hp, :][:, :, None].to_broadcast([P, SEQS, STEPS]), ALU.mult)
                ks = KCT[0:NS, TILES, :].rearrange("p (h d) -> p h d", h=HC)
                ve.tensor_tensor(ks, ks, COL[0:NS, 60 + HB:72][:, :, None].to_broadcast([NS, HC, DKC]), ALU.mult)\
                    .then_inc(s_kws, 1)
                wait(t["sintra"])
                wait(t["ses"])
                for h2 in range(2):
                    last = ve.tensor_tensor(WSM[0:NS, h2:HC:2, :], ES[0:NS, h2:HC:2, :],
                                            Q[0:NS, h2, 0:2 * NS].rearrange("p (h n) -> p h n", h=2), ALU.mult)
                last.then_inc(s_sw, 1)
                wait(t["num"])
                den = TB[:, 1, 0:HC * NS].rearrange("p (h n) -> p h n", h=HC)
                link(ve.scalar_tensor_tensor(ARG, den, -1.0, EMS, ALU.mult, ALU.max))
                link(ve.tensor_tensor(ARG, ARG, den, ALU.max))
                link(ve.reciprocal(ARG, ARG))
                link(ve.tensor_tensor(ES, TB[:, 0, 0:HC * NS].rearrange("p (h n) -> p h n", h=HC), ARG, ALU.mult))
                ve.tensor_tensor(YC[:, :, NP:T], YC[:, :, NP:T], ES, ALU.mult).then_inc(s_yc, 1)
                wait(c0)
                for hp in range(2):
                    for h2 in range(2):
                        h = 2 * hp + h2
                        ve.tensor_tensor(VBLK[0:NS, h2, :, :],
                                         TV2[0:NS, TILES, h * P:(h + 1) * P][:, None, :].to_broadcast([NS, SEQS, P]),
                                         own_seq[:, :, None].to_broadcast([NS, SEQS, P]), ALU.mult).then_inc(s_vblk, 1)
                    dec = WIB[:, hp, STEPS - 1:NS:STEPS]
                    link(ve.tensor_tensor(CS[:, hp], CS[:, hp], dec[:, :, None].to_broadcast([P, SEQS, P]), ALU.mult))
                    p = mine()
                    ve.tensor_tensor(CS[:, hp].rearrange("p (a s) v -> p a (s v)", a=2),
                                     CS[:, hp].rearrange("p (a s) v -> p a (s v)", a=2),
                                     G[:, 2 * p:2 * p + 2, :], ALU.add).then_inc(s_dr[p], 1)
                    ve.wait_ge(s_dr[p], un.d[p].value())
                    ve.sem_inc(s_stn, 1)
                link(ve.tensor_tensor(N0[:], N0[:], WIB[:, :, STEPS - 1:NS:STEPS], ALU.mult))
                p = mine()
                ve.tensor_tensor(N0[:], N0[:], G[:, 2 * p, 0:2 * SEQS].rearrange("p (h s) -> p h s", h=2), ALU.add)\
                    .then_inc(s_dr[p], 1)
                ve.wait_ge(s_dr[p], un.d[p].value())
                ve.sem_inc(s_stn, 1)
                ve.sem_inc(s_lff, 1)
                un.take(13)
                for m in range(8):
                    p = mine()
                    wait(t["rtn"])
                    drained(ve.reciprocal(RT[:, m % 2, :], RT[:, m % 2, :]), p)
                    ve.wait_ge(s_dr[p], un.d[p].value())
                    ve.scalar_tensor_tensor(QKB[:, m, :], QKB[:, m, :], GQK[:, m // 4:m // 4 + 1], RT[:, m % 2, :],
                                            ALU.mult, ALU.mult).then_inc(s_qkr, 1)
                wait(t["qkr"], 8)
                for h in range(HB):
                    r = slice(64 * (h % 2), 64 * (h % 2) + 64)
                    last = ve.tensor_copy(QS[r, h // 2, :, h, :], by_seq(QKB[r, h // 2, NP:T]))
                last.then_inc(s_qs, 1)
                for hp in range(4):
                    un.take(2)
                    for q in range(2):
                        ve.wait_ge(s_dr[q], un.d[q].value())
                    for n in range(8 + 1):
                        if n < 8:
                            it, i, h = hp * 8 + n, n % TILES, 2 * hp + n // TILES
                            w = (i + 1) * P
                            if it >= 2:
                                wait(t["pt"])
                            wait(t["sc"])
                            apart(ve)
                            link(ve.tensor_tensor_reduce(SCR[:, it % 2, 0:w], Q[:, it % 2, 0:w], NF[:, h % 4, 0:w], 1.0,
                                                         -BIG, ALU.add, ALU.max, SMALL[:, 18 + it % 2:19 + it % 2]))
                            ve.tensor_scalar(SMALL[:, 16 + it % 2:17 + it % 2], SMALL[:, 18 + it % 2:19 + it % 2], -1.0,
                                             None, ALU.mult).then_inc(s_max, 1)
                        if n >= 1:
                            it = hp * 8 + n - 1
                            w = ((n - 1) % TILES + 1) * P
                            wait(t["exp"])
                            s1 = SMALL[:, 20 + it % 2:21 + it % 2]
                            link(ve.reciprocal(s1, s1))
                            ve.tensor_scalar(SCR[:, it % 2, 0:w], SCR[:, it % 2, 0:w], s1, None, ALU.mult).then_inc(s_p, 1)
                    un.take()
                wait(t["pt"], 2)
                for g in range(2):
                    ve.tensor_tensor(DIAG[0:NS, g, :].rearrange("p (s h q) -> p s h q", s=4, h=HB),
                                     new_seq[:, 4 * g:4 * g + 4][:, :, None, None].to_broadcast([NS, 4, HB, STEPS]),
                                     COL[0:NS, 72:72 + HB][:, None, :, None].to_broadcast([NS, 4, HB, STEPS]),
                                     ALU.mult).then_inc(s_ln, 1)
                for g in range(2):
                    wait(lf, 32)
                    link(ve.tensor_tensor_scan(FB[:, 0:PAST], ones[:, 0:1].to_broadcast([P, PAST]), LFR, 0.0,
                                               ALU.mult, ALU.add))
                    if g == 0:
                        ve.sem_inc(s_lff, 1)
                    p = mine()
                    drained(ve.scalar_tensor_tensor(FB[:, PAST:PAST + NS], G[:, 2 * p, 0:NS], FB[:, PAST - 1:PAST],
                                                    new_mask[:, g, :], ALU.add, ALU.subtract), p)
                    ve.wait_ge(s_dr[p], un.d[p].value())
                    wait(t["ss"])
                    if g == 1:
                        un.take(2)
                        ve.wait_ge(s_unit, un.u.value())
                    ve.scalar_tensor_tensor(SSC[:, 0:PAST].rearrange("p (a n) -> p a n", a=2),
                                            FB[:, 0:PAST].rearrange("p (a n) -> p a n", a=2), -1.0, Q[:, :, :],
                                            ALU.mult, ALU.add)
                    link(ve.scalar_tensor_tensor(SSC[:, PAST:PAST + NS], FB[:, PAST:PAST + NS], -1.0, TB[:, 0, 0:NS],
                                                 ALU.mult, ALU.add))
                    link(ve.tensor_reduce(SMALL[:, 26:27], SSC, AX.X, ALU.max))
                    ve.tensor_scalar(SMALL[:, 24:25], SMALL[:, 26:27], -1.0, None, ALU.mult).then_inc(s_smx, 1)
                    wait(t["sex"])
                    link(ve.reciprocal(SMALL[:, 27:28], SMALL[:, 25:26]))
                    ve.tensor_scalar(SSC, SSC, SMALL[:, 27:28], None, ALU.mult).then_inc(s_ps, 1)
                un.take(2)
                for g in range(2):
                    wait(t["pv"])
                    for h2 in range(2):
                        r = slice(64 * h2, 64 * h2 + 64)
                        src = TB[r, 1, 0:P].rearrange("p (s k c) -> p s k c", s=4, k=4)[:, :, :, 4 * h2:4 * h2 + 4]
                        dst = YB[r, :, NP + 16 * g:NP + 16 * g + 16].rearrange("p k (s q) -> p s k q", s=4)
                        last = ve.tensor_copy(dst, src)
                    last.then_inc(s_pvc, 1)
                with repeat(ve, KD, un.strides(6) | {st: 1, t["m"]: 1}) as m:
                    un.take(3)
                    acc = ZT[:, 0, :]
                    for b in range(3):
                        p = mine()
                        if b == 0:
                            ve.wait_ge(s_dr[(p + 1) % 2], un.d[(p + 1) % 2].value())
                        z = ZT[:, 0 if b == 0 else 1, :]
                        ve.tensor_tensor(halves(z), both(p), halves(GT[:, b, :]), ALU.mult).then_inc(s_dr[p], 1)
                        ve.wait_ge(s_dr[p], un.d[p].value())
                        if b == 1:
                            link(ve.tensor_tensor(acc, acc, z, ALU.add))
                        if b == 2:
                            o = MT[:, bass.ds(m, 1), :].rearrange("p a n -> p (a n)")
                            ve.tensor_tensor(o, acc, z, ALU.add).then_inc(s_m, 1)
                            wait(t["m"])
                ve.sem_inc(s_smallf, 1)
                add_to_x(24 + 16)
                ffn(2, STEPS_L - FFN_STEPS)


_OUTS = dict(y=(P, KD, T), k=(L, P, 4, T), v=(L, T, 512), logf=(L, HB, T), m=(L, HC, NS + 1),
             C_prompt=(L, P, 2, P), n_prompt=(L, P, 2), C_sample=(L, 2, P, SEQS, P), n_sample=(L, P, 2, SEQS),
             chunk_v=(L, NS, 512))


def lay_out(x):
    a = {k: np.asarray(v) for k, v in x.items()}

    def blocks(w, k):
        return w.reshape(L, k, P, -1).transpose(0, 2, 1, 3)

    def steps(w, k, n):
        b = blocks(w, k)
        s = b.shape[3] // n
        return b.reshape(L, P, k, s, n).transpose(0, 3, 1, 2, 4).reshape(L * s, P, k * n)

    tokens = np.concatenate([a["x_prompt"][0], a["x_sample"].reshape(NS, D)])
    cond = np.concatenate([a["c_prompt"], a["c_sample"]])
    w_in = a["w_in"]
    cut = np.cumsum([0, 512, 512, 512, 512, 512, HB, 256, 256, 512, HC, HC, 512, 3 * D])
    ua, va, qb, kb, vb, fb, qc, kc, vc, ic, fc, oc, gt = (w_in[:, :, cut[i]:cut[i + 1]] for i in range(13))
    up = a["w_ff_up"].reshape(L, 2, KD, P, 2, KF // 2, 2, P).transpose(0, 1, 5, 3, 6, 4, 2, 7)
    down = a["w_ff_down"].reshape(L, 2, KF, P, DOWN_STEPS, 2, P).transpose(0, 1, 4, 3, 5, 2, 6)
    part = (slice(0, FF_PART[0]), slice(FF_PART[0], KF))
    gates = gt.reshape(L, KD, P, 3, KD, P).transpose(0, 4, 2, 1, 3, 5)
    branch = a["w_branch"].reshape(L, 3, 4, P, KD, P).transpose(0, 4, 3, 1, 2, 5)
    zero = np.zeros((L, D, 20), w_in.dtype)
    b_rows = np.zeros((L, 44, 1), w_in.dtype)
    b_rows[:, 0:HB, 0], b_rows[:, HB:ROWS, 0], b_rows[:, 32 + HB:44, 0] = a["b_fb"], a["b_fc"], a["b_ic"]
    m0 = np.zeros((L, ROWS, SEQS), a["state_m"].dtype)
    m0[:, HB:] = a["state_m"].transpose(0, 2, 1)
    w_s = a["w_s"].transpose(0, 3, 1, 2)
    pool = a["cache_k"].shape[1]
    laid = dict(
        consts=constants(),
        x=tokens.T.reshape(KD, P, T).transpose(1, 0, 2),
        c=cond.T.reshape(KD, P, C).transpose(1, 0, 2),
        w_ada=steps(a["w_ada"], KD, 512),
        w_up=up.reshape(L * KF, P, SLOT),
        w_down0=down[..., part[0], :].reshape(L * 2 * DOWN_STEPS, P, 2 * FF_PART[0] * P),
        w_down1=down[..., part[1], :].reshape(L * 2 * DOWN_STEPS, P, 2 * FF_PART[1] * P),
        w_in=np.stack([steps(w, KD, 512) for w in (ua, va, np.concatenate([qc, kc], 2), vc, oc, qb, kb, vb)], 1)
        .reshape(L * 8, P, SLOT),
        w_rows=blocks(np.concatenate([fb, fc, zero, zero[:, :, :HB], ic], 2), KD),
        w_gate=gates.reshape(L * KD, P, KD * 3 * P),
        w_branch=branch.reshape(L * KD, P, 12 * P),
        w_out=steps(a["w_out"], KD, 512),
        b_ada=a["b_ada"].reshape(L, 9 * KD, P).transpose(0, 2, 1),
        g_norm=a["g_norm"].reshape(L, 3, KD, P).transpose(0, 3, 1, 2),
        g_va=a["g_va"], b_s=a["b_s"], w_s=w_s,
        w_s_new=np.tile(w_s[:, 0:STEPS, :, 0:STEPS], (1, SEQS, 1, SEQS)),
        b_rows=b_rows,
        g_qk=np.tile(np.stack([a["g_qb"], a["g_kb"]], 2), (1, 2, 1)),
        m0=m0,
        n0=a["state_n"].reshape(L, SEQS, 2, P).transpose(0, 3, 2, 1),
        C0=a["state_C"].reshape(L, SEQS, 2, 2, P, DKC).transpose(0, 3, 5, 2, 1, 4).reshape(L, P, 2, SEQS, P),
        page_table=a["page_table"].reshape(1, SEQS * PAGES),
        cache_k=a["cache_k"].reshape(L * pool, PAGE, 4, P).transpose(0, 3, 2, 1).reshape(L * pool, P, 512),
        cache_v=a["cache_v"].reshape(L * pool, PAGE, 512),
        cache_f=a["cache_logf"].reshape(L * pool, PAGE, HB).transpose(0, 2, 1),
    )
    return {k: np.ascontiguousarray(v) for k, v in laid.items()}


def results(o):
    y = o["y"].transpose(1, 0, 2).reshape(D, T).T
    k = o["k"].transpose(0, 3, 2, 1).reshape(L, T, HB, DB)
    v = o["v"].reshape(L, T, HB, DB)
    lf = o["logf"].transpose(0, 2, 1)
    cp = o["C_prompt"].reshape(L, 2, DKC, 2, P).transpose(0, 3, 1, 4, 2).reshape(L, 1, HC, DVC, DKC)
    np_ = o["n_prompt"].reshape(L, 2, DKC, 2).transpose(0, 3, 1, 2).reshape(L, 1, HC, DKC)
    cs = o["C_sample"].reshape(L, 2, 2, DKC, SEQS, P).transpose(0, 4, 1, 2, 5, 3).reshape(L, SEQS, HC, DVC, DKC)
    ns = o["n_sample"].reshape(L, 2, DKC, 2, SEQS).transpose(0, 4, 3, 1, 2).reshape(L, SEQS, HC, DKC)
    out = (y[:NP].reshape(1, NP, D), y[NP:].reshape(SEQS, STEPS, D),
           k[:, :NP].reshape(L, 1, NP, HB, DB), v[:, :NP].reshape(L, 1, NP, HB, DB), lf[:, :NP].reshape(L, 1, NP, HB),
           cp, np_, o["m"][:, :, 0].reshape(L, 1, HC),
           k[:, NP:].reshape(L, SEQS, STEPS, HB, DB), v[:, NP:].reshape(L, SEQS, STEPS, HB, DB),
           lf[:, NP:].reshape(L, SEQS, STEPS, HB), cs, ns, o["m"][:, :, STEPS::STEPS].transpose(0, 2, 1),
           o["chunk_v"].reshape(L, SEQS, STEPS, 512))
    return tuple(np.ascontiguousarray(r) for r in out)


def kernel(**inputs):
    import concourse.bacc as bacc
    from concourse.bass_utils import run_bass_kernel_spmd

    arrays = lay_out(inputs)
    nc = bacc.Bacc("TRN2", target_bir_lowering=False, num_devices=1)
    d = {k: nc.dram_tensor("in_" + k, v.shape, mybir.dt.from_np(v.dtype), kind="ExternalInput").ap() for k, v in arrays.items()}
    d["outs"] = {k: nc.dram_tensor("out_" + k, s, F32, kind="ExternalOutput").ap() for k, s in _OUTS.items()}
    build(nc, d, d["outs"])
    r = run_bass_kernel_spmd(nc, [{"in_" + k: v for k, v in arrays.items()}], core_ids=[0]).results[0]
    return results({k: np.asarray(r["out_" + k]) for k in _OUTS})
```
